# Optimizing a Trainium2 kernel written in Bass

```python
import jax, jax.numpy as jnp
from jax import lax
import numpy as np

D_MODEL = 1024
BATCH = 1
SEQ = 512
DEPTH = 1
DEC_BATCH = 1
DEC_SEQ = 32
PAST_LEN = 512

CHUNK = 64
MIX_WIDTH = D_MODEL
WIDTH_A = MIX_WIDTH // 2
WIDTH_B = MIX_WIDTH - WIDTH_A
IN_COLS = 3 * WIDTH_A + 2 * WIDTH_B
CONV_A = 3
CONV_B = 31
N_KEYS = 128
N_EXPERTS = N_KEYS * N_KEYS
PEER_HEADS = 8
PEER_TOPK = 16
D_KEY = 128
PEER_BLOCK = 128
EPS = 1e-6

kernel_name = 'hymba_style_conv_hybrid_peer_stream_step'

def rmsnorm(x, g):
    xf = x.astype(jnp.float32)
    y = xf * lax.rsqrt(jnp.mean(xf * xf, axis=-1, keepdims=True) + EPS)
    return (y * g.astype(jnp.float32)).astype(x.dtype)

def layernorm(x, g, b):
    xf = x.astype(jnp.float32)
    mu = jnp.mean(xf, axis=-1, keepdims=True)
    xc = xf - mu
    y = xc * lax.rsqrt(jnp.mean(xc * xc, axis=-1, keepdims=True) + EPS)
    return (y * g.astype(jnp.float32) + b.astype(jnp.float32)).astype(x.dtype)

def causal_dwconv(hist, x, w):
    k = w.shape[0]
    xp = jnp.concatenate([hist.astype(x.dtype), x], axis=1)
    y = lax.conv_general_dilated(xp, w[:, None, :].astype(x.dtype), window_strides=(1,), padding='VALID',
                                 dimension_numbers=('NWC', 'WIO', 'NWC'), feature_group_count=x.shape[-1])
    return y, xp[:, -(k - 1):]

def token_mixers(xn, hist_a, hist_b, w_in, conv_a_w, conv_b_w, conv_b_b, conv_norm_g, conv_norm_b,
                 out_norm_a_g, out_norm_b_g, w_out):
    proj = jnp.einsum('bld,de->ble', xn, w_in)
    h_a, c_a, b_a, v_b, g_b = jnp.split(
        proj, [WIDTH_A, 2 * WIDTH_A, 3 * WIDTH_A, 3 * WIDTH_A + WIDTH_B], axis=-1)
    conv_out_a, new_a = causal_dwconv(hist_a, c_a * h_a, conv_a_w)
    y_a = rmsnorm(b_a * conv_out_a, out_norm_a_g)
    glu = v_b * jax.nn.sigmoid(g_b)
    conv_out_b, new_b = causal_dwconv(hist_b, glu, conv_b_w)
    z = jax.nn.silu(layernorm(conv_out_b + conv_b_b.astype(glu.dtype), conv_norm_g, conv_norm_b))
    y_b = rmsnorm(z, out_norm_b_g)
    y = jnp.einsum('ble,ed->bld', jnp.concatenate([y_a, y_b], axis=-1), w_out)
    return y, new_a, new_b

def peer_tokens(xt, w_q, sub_keys, u_experts, v_experts):
    q = jnp.einsum('td,de->te', xt, w_q).reshape(xt.shape[0], PEER_HEADS, 2, D_KEY)
    s = jnp.einsum('thpc,hpkc->thpk', q, sub_keys).astype(jnp.float32)
    s1, i1 = lax.top_k(s[:, :, 0], PEER_TOPK)
    s2, i2 = lax.top_k(s[:, :, 1], PEER_TOPK)
    cand = (s1[..., :, None] + s2[..., None, :]).reshape(xt.shape[0], PEER_HEADS, PEER_TOPK * PEER_TOPK)
    top_s, j = lax.top_k(cand, PEER_TOPK)
    e = (jnp.take_along_axis(i1, j // PEER_TOPK, axis=-1) * N_KEYS
         + jnp.take_along_axis(i2, j % PEER_TOPK, axis=-1))
    gate = jax.nn.softmax(top_s, axis=-1).astype(xt.dtype)
    u = jnp.take(u_experts, e, axis=0)
    v = jnp.take(v_experts, e, axis=0)
    act = jax.nn.gelu(jnp.einsum('td,thkd->thk', xt, u), approximate=False)
    return jnp.einsum('thk,thkd->td', gate * act, v)

def peer(xn, w_q, sub_keys, u_experts, v_experts):
    n, l, d = xn.shape
    t = n * l
    xt = xn.reshape(t, d)
    fn = lambda blk: peer_tokens(blk, w_q, sub_keys, u_experts, v_experts)
    if t % PEER_BLOCK == 0 and t > PEER_BLOCK:
        out = lax.map(fn, xt.reshape(t // PEER_BLOCK, PEER_BLOCK, d)).reshape(t, d)
    else:
        out = fn(xt)
    return out.reshape(n, l, d)

def trunk(x, hist_a, hist_b, norm_mix_g, w_in, conv_a_w, conv_b_w, conv_b_b, conv_norm_g, conv_norm_b,
          out_norm_a_g, out_norm_b_g, w_out, norm_ffn_g, w_q, sub_keys, u_experts, v_experts, final_norm_g):
    new_a, new_b = [], []
    for layer in range(DEPTH):
        y, ha, hb = token_mixers(rmsnorm(x, norm_mix_g[layer]), hist_a[layer], hist_b[layer], w_in[layer],
                                 conv_a_w[layer], conv_b_w[layer], conv_b_b[layer], conv_norm_g[layer],
                                 conv_norm_b[layer], out_norm_a_g[layer], out_norm_b_g[layer], w_out[layer])
        h = x + y
        x = h + peer(rmsnorm(h, norm_ffn_g[layer]), w_q[layer], sub_keys[layer], u_experts[layer], v_experts[layer])
        new_a.append(ha)
        new_b.append(hb)
    return rmsnorm(x, final_norm_g), jnp.stack(new_a), jnp.stack(new_b)

def setup_inputs(seed: int = 0) -> dict:
    key = jax.random.key(seed)
    ks = jax.random.split(key, 20)
    f32 = jnp.float32

    def nrm(k, shape, scale):
        return jax.random.normal(k, shape, f32) * scale

    def gain(k, shape):
        return 1.0 + 0.05 * jax.random.normal(k, shape, f32)

    return {
        'x_prompt': nrm(ks[0], (BATCH, SEQ, D_MODEL), 1.0),
        'x_sample': nrm(ks[1], (DEC_BATCH, DEC_SEQ, D_MODEL), 1.0),
        'cache_conv_a': nrm(ks[2], (DEPTH, DEC_BATCH, CONV_A - 1, WIDTH_A), 1.0),
        'cache_conv_b': nrm(ks[3], (DEPTH, DEC_BATCH, CONV_B - 1, WIDTH_B), 1.0),
        'norm_mix_g': gain(ks[4], (DEPTH, D_MODEL)),
        'w_in': nrm(ks[5], (DEPTH, D_MODEL, IN_COLS), D_MODEL ** -0.5),
        'conv_a_w': nrm(ks[6], (DEPTH, CONV_A, WIDTH_A), CONV_A ** -0.5),
        'conv_b_w': nrm(ks[7], (DEPTH, CONV_B, WIDTH_B), CONV_B ** -0.5),
        'conv_b_b': nrm(ks[8], (DEPTH, WIDTH_B), 0.02),
        'conv_norm_g': gain(ks[9], (DEPTH, WIDTH_B)),
        'conv_norm_b': nrm(ks[10], (DEPTH, WIDTH_B), 0.02),
        'out_norm_a_g': gain(ks[11], (DEPTH, WIDTH_A)),
        'out_norm_b_g': gain(ks[12], (DEPTH, WIDTH_B)),
        'w_out': nrm(ks[13], (DEPTH, MIX_WIDTH, D_MODEL), MIX_WIDTH ** -0.5),
        'norm_ffn_g': gain(ks[14], (DEPTH, D_MODEL)),
        'w_q': nrm(ks[15], (DEPTH, D_MODEL, PEER_HEADS * 2 * D_KEY), D_MODEL ** -0.5),
        'sub_keys': nrm(ks[16], (DEPTH, PEER_HEADS, 2, N_KEYS, D_KEY), D_KEY ** -0.5),
        'u_experts': nrm(ks[17], (DEPTH, N_EXPERTS, D_MODEL), D_MODEL ** -0.5),
        'v_experts': nrm(ks[18], (DEPTH, N_EXPERTS, D_MODEL), PEER_HEADS ** -0.5),
        'final_norm_g': gain(ks[19], (D_MODEL,)),
    }

def reference(x_prompt, x_sample, cache_conv_a, cache_conv_b, norm_mix_g, w_in, conv_a_w, conv_b_w, conv_b_b,
              conv_norm_g, conv_norm_b, out_norm_a_g, out_norm_b_g, w_out, norm_ffn_g, w_q, sub_keys,
              u_experts, v_experts, final_norm_g):
    zeros_a = jnp.zeros((DEPTH, x_prompt.shape[0], CONV_A - 1, WIDTH_A), x_prompt.dtype)
    zeros_b = jnp.zeros((DEPTH, x_prompt.shape[0], CONV_B - 1, WIDTH_B), x_prompt.dtype)
    y_prompt, conv_a_prompt, conv_b_prompt = trunk(
        x_prompt, zeros_a, zeros_b, norm_mix_g, w_in, conv_a_w, conv_b_w, conv_b_b, conv_norm_g, conv_norm_b,
        out_norm_a_g, out_norm_b_g, w_out, norm_ffn_g, w_q, sub_keys, u_experts, v_experts, final_norm_g)
    y_sample, conv_a_sample, conv_b_sample = trunk(
        x_sample, cache_conv_a, cache_conv_b, norm_mix_g, w_in, conv_a_w, conv_b_w, conv_b_b, conv_norm_g,
        conv_norm_b, out_norm_a_g, out_norm_b_g, w_out, norm_ffn_g, w_q, sub_keys, u_experts, v_experts,
        final_norm_g)
    return (y_prompt, y_sample, conv_a_prompt, conv_b_prompt, conv_a_sample, conv_b_sample)


_drawn_inputs = setup_inputs


def setup_inputs(seed=0):
    import zlib

    import numpy as np

    out = dict(_drawn_inputs(seed))
    spreads = {}
    factors = {'conv_norm_b': 3.316}
    for name, (base, spread) in spreads.items():
        noise = np.random.default_rng([zlib.crc32(name.encode()), seed]).standard_normal(out[name].shape)
        drawn = base * np.exp(spread * noise) if base else spread * noise
        out[name] = __import__('jax').numpy.asarray(drawn.astype(out[name].dtype))
    for name, factor in factors.items():
        out[name] = (out[name] * factor).astype(out[name].dtype)
    return out
```

```python
from contextlib import ExitStack

import concourse.bass as bass
from concourse import mybir

F32 = mybir.dt.float32
F32R = mybir.dt.float32r
U32 = mybir.dt.uint32
I32 = mybir.dt.int32
ALU = mybir.AluOpType
ACT = mybir.ActivationFunctionType
AX_X = mybir.AxisListType.X

P = 128
D = 1024
KC = D // P
T_PROMPT, T_SAMPLE = 512, 32
T = T_PROMPT + T_SAMPLE
HALF = T // 2
WIDTH = 512
WC = WIDTH // P
TAPS_A, TAPS_B = 3, 31
HIST_A, HIST_B = TAPS_A - 1, TAPS_B - 1
PAD_A = 2 * HIST_A + T
PAD_B = 2 * HIST_B + T
HEADS, TOPK, NKEYS = 8, 16, 128
TILES = (T + P - 1) // P
EPS = 1e-6

RING = 4
N_IN, N_OUT, N_Q = 5 * WC, KC, 2 * HEADS
N_U = NKEYS
GROUP = 8
GROUPS = NKEYS // GROUP
N_V = GROUPS * KC
FIRST_OUT = N_IN
FIRST_Q = FIRST_OUT + N_OUT
FIRST_U = FIRST_Q + N_Q
FIRST_V = FIRST_U + N_U
N_UNITS = FIRST_V + N_V

GT = 32
GTS = T // GT
BATCH = 4
BATCHES = GT // BATCH
U_BEFORE = 7
U_AFTER = N_U // RING - U_BEFORE - GTS

PARAMS = {}
N_PARAMS = 0
for _name, _n in (("mix_g", KC), ("ffn_g", KC), ("final_g", KC), ("conv_a_w", WC * TAPS_A),
                  ("conv_b_w", WC * TAPS_B), ("conv_b_b", WC), ("conv_norm_g", WC), ("conv_norm_b", WC),
                  ("out_a_g", WC), ("out_b_g", WC), ("hist_a", WC * HIST_A), ("hist_b", WC * HIST_B)):
    PARAMS[_name] = N_PARAMS
    N_PARAMS += _n
CACHE_A = WC * 2 * HIST_A
N_CACHE = CACHE_A + WC * 2 * HIST_B


def build(nc, stream, x_t, params, sub_keys, y_t, caches):
    gates_dram = nc.dram_tensor("gates_dram", (GTS, P, NKEYS, GT), F32, kind="Internal").ap()
    acts_dram = nc.dram_tensor("acts_dram", (N_U, P, T), F32, kind="Internal").ap()

    with ExitStack() as ctx:
        def sb_in(stack, name, shape, dt=F32):
            return stack.enter_context(nc.sbuf_tensor(name, shape, dt))

        def sb(name, shape, dt=F32):
            return sb_in(ctx, name, shape, dt)

        def sem(name):
            return ctx.enter_context(nc.semaphore(name))

        par = sb("par", [P, N_PARAMS])
        hid = sb("hid", [P, KC, T])
        mov_hi = sb("mov_hi", [P, KC, T], F32R)
        mov_lo = sb("mov_lo", [P, KC, T], F32R)
        raw = sb("raw", [P, RING, KC * P])
        w_hi = sb("w_hi", [P, RING, KC * P], F32R)
        w_lo = sb("w_lo", [P, RING, KC * P], F32R)
        ones = sb("ones", [P, P])
        eps = sb("eps", [P, 1])
        iota_i = sb("iota_i", [P, P], I32)
        iota = sb("iota", [P, P])
        ident = sb("ident", [P, P])
        std = sb("std", [P, T])
        rstd = sb("rstd", [P, T])
        cache_out = sb("cache_out", [P, N_CACHE])

        mixer = ExitStack()
        proj = sb_in(mixer, "proj", [P, N_IN, T])
        pad_a = sb_in(mixer, "pad_a", [P, WC, PAD_A])
        pad_b = sb_in(mixer, "pad_b", [P, WC, PAD_B])
        conv = sb_in(mixer, "conv", [P, PAD_B])
        nrm = sb_in(mixer, "nrm", [P, KC, T])
        sq = sb_in(mixer, "sq", [P, KC, T])
        mixer.close()

        act_ring = sb("act_ring", [P, 2, T])
        route = ExitStack()
        keys = sb_in(route, "keys", [P, 2 * HEADS, NKEYS])
        ij = sb_in(route, "ij", [P, 2, TILES, HEADS, TOPK])
        tops = sb_in(route, "tops", [P, TILES * HEADS, TOPK])
        gate = sb_in(route, "gate", [P, TILES * HEADS, TOPK])
        gate_sum = sb_in(route, "gate_sum", [P, TILES * HEADS])
        ij_t = sb_in(route, "ij_t", [P, 2, T])
        gate_t = sb_in(route, "gate_t", [P, T])
        gate_hi = sb_in(route, "gate_hi", [P, T], F32R)
        gate_lo = sb_in(route, "gate_lo", [P, T])
        topk = ExitStack()
        scores = sb_in(topk, "scores", [P, HEADS, TILES, 2 * NKEYS])
        q_ring = sb_in(topk, "q_ring", [P, RING, T])
        cur = sb_in(topk, "cur", [P, TILES, 2 * NKEYS])
        best = sb_in(topk, "best", [P, TILES, 2, TOPK])
        best_at = sb_in(topk, "best_at", [P, TILES, 2, TOPK], U32)
        best_at_f = sb_in(topk, "best_at_f", [P, TILES, 2, TOPK])
        top = sb_in(topk, "top", [P, TILES, TOPK])
        pair = sb_in(topk, "pair", [P, TILES, TOPK, TOPK])
        pair_at = sb_in(topk, "pair_at", [P, TILES, TOPK], U32)
        rank_u = sb_in(topk, "rank_u", [P, 2, TILES, TOPK], U32)
        rank = sb_in(topk, "rank", [P, 2, TILES, TOPK])
        topk.close()
        build_g = ExitStack()
        gates = sb_in(build_g, "gates", [P, 2, NKEYS, GT])
        hot_j = sb_in(build_g, "hot_j", [P, 2, BATCH, P], F32R)
        hot_i = sb_in(build_g, "hot_i", [P, 2, BATCH, P])
        gated_hi = sb_in(build_g, "gated_hi", [P, 2, BATCH, P], F32R)
        gated_lo = sb_in(build_g, "gated_lo", [P, 2, BATCH, P], F32R)
        build_g.close()
        route.close()

        values = ExitStack()
        acts_in = sb_in(values, "acts_in", [P, 2, 2, T])
        gates_in = sb_in(values, "gates_in", [P, 2, GTS, GROUP // 2, GT])
        prod = sb_in(values, "prod", [P, T])
        prod_hi = sb_in(values, "prod_hi", [P, 2, GROUP, T], F32R)
        prod_lo = sb_in(values, "prod_lo", [P, 2, GROUP, T], F32R)
        values.close()

        final = ExitStack()
        sq_f = sb_in(final, "sq_f", [P, KC, T])
        y_sb = sb_in(final, "y_sb", [P, KC, T])
        final.close()

        ps_unit = ctx.enter_context(nc.psum_tensor("ps_unit", [P, 4, 512], F32))
        ps_misc = ctx.enter_context(nc.psum_tensor("ps_misc", [P, 4, 512], F32))

        params_in = sem("params_in")
        x_in = sem("x_in")
        keys_in = sem("keys_in")
        raw_in = [sem(f"raw_in{s}") for s in range(RING)]
        hi_made = sem("hi_made")
        lo_made = sem("lo_made")
        unit_done = sem("unit_done")
        act_took = sem("act_took")
        dve_took = sem("dve_took")
        consts_made = sem("consts_made")
        iota_made = sem("iota_made")
        ident_made = sem("ident_made")
        sq_made = sem("sq_made")
        sum_done = sem("sum_done")
        std_made = sem("std_made")
        nrm_made = sem("nrm_made")
        mov_hi_made = sem("mov_hi_made")
        mov_lo_made = sem("mov_lo_made")
        conv_b_made = sem("conv_b_made")
        ya_made = sem("ya_made")
        centred = sem("centred")
        scaled_b = sem("scaled_b")
        silu_made = sem("silu_made")
        cache_made = sem("cache_made")
        cache_saved = sem("cache_saved")
        scores_done = sem("scores_done")
        scores_took = sem("scores_took")
        shifted = sem("shifted")
        exp_made = sem("exp_made")
        gate_made = sem("gate_made")
        turned = sem("turned")
        turned_took = sem("turned_took")
        hot_made = sem("hot_made")
        g_done = sem("g_done")
        g_took = sem("g_took")
        g_saved = [sem(f"g_saved{s}") for s in range(2)]
        act_saved = [sem(f"act_saved{s}") for s in range(RING)]
        acts_back = [sem(f"acts_back{s}") for s in range(2)]
        gates_back = [sem(f"gates_back{s}") for s in range(2)]
        prod_made = sem("prod_made")
        dve_step = sem("dve_step")
        y_made = sem("y_made")
        y_saved = sem("y_saved")

        block = ctx.enter_context(nc.Block())

        def par_col(name, i, n=1):
            return par[:, PARAMS[name] + i:PARAMS[name] + i + n]

        def halves(ap):
            return ap.rearrange("p (a b) -> p a b", a=2)

        def unit_psum(j):
            return ps_unit[:, 2 * (j % 2):2 * (j % 2) + 2, 0:HALF]

        def sum_psum(pair_of_banks):
            return ps_misc[:, 2 * pair_of_banks:2 * pair_of_banks + 2, 0:HALF]


        @block.sync
        def _(sp):
            def load(lap, j):
                if not (isinstance(lap, int) and lap == 0):
                    sp.wait_ge(hi_made, RING * (lap - 1) + j + 1)
                    sp.wait_ge(lo_made, RING * (lap - 1) + j + 1)
                src = stream[bass.ds(RING * lap + j, 1)].rearrange("a p n -> p (a n)")
                sp.dma_start(raw[:, j, :], src).then_inc(raw_in[j], 16)

            def load_acts(half, q):
                for n in (2 * q, 2 * q + 1):
                    sp.wait_ge(act_saved[n], 16 * (half + 1))
                acts = acts_dram[bass.ds(4 * half + 2 * q, 2)].rearrange("e p t -> p e t")
                sp.dma_start(acts_in[:, q], acts).then_inc(acts_back[q], 16)

            def load_gates(pair_lap, s):
                g = gates_dram[:, :, bass.ds(4 * (2 * pair_lap + s), 4), :].rearrange("g p e t -> p g (e t)")
                sp.dma_start(gates_in[:, s].rearrange("p g e t -> p g (e t)"), g).then_inc(gates_back[s], 16)

            sp.dma_start(hid[:], x_t).then_inc(x_in, 16)
            sp.dma_start(par[:], params).then_inc(params_in, 16)
            for j in range(RING):
                load(0, j)
            with sp.Fori(1, FIRST_V // RING - 4) as lap:
                for j in range(RING):
                    load(lap, j)
            sp.wait_ge(g_saved[0], 16 * ((GTS + 1) // 2))
            sp.wait_ge(g_saved[1], 16 * (GTS // 2))
            for s in range(2):
                load_gates(0, s)
                load_acts(0, s)
            with sp.Fori(FIRST_V // RING - 4, FIRST_V // RING) as lap:
                for j in range(RING):
                    load(lap, j)
            sp.wait_ge(prod_made, 2)
            load_acts(1, 0)

            def value_lap(pair_lap, s, gates_too=True):
                v = 8 * pair_lap + 4 * s
                sp.wait_ge(prod_made, v + 4)
                if gates_too:
                    load_gates(pair_lap + 1, s)
                load_acts(2 * pair_lap + s + 1, 1)
                for j in range(RING):
                    if j == 2 and gates_too:
                        sp.wait_ge(prod_made, v + 6)
                        load_acts(2 * pair_lap + s + 2, 0)
                    load(2 * pair_lap + s + FIRST_V // RING, j)

            with sp.Fori(0, GROUPS - 1) as pair_lap:
                value_lap(pair_lap, 0)
                value_lap(pair_lap, 1)
            value_lap(GROUPS - 1, 0, gates_too=False)
            for j in range(RING):
                load(N_UNITS // RING - 1, j)
            sp.wait_ge(y_saved, 16 * KC)
            sp.wait_ge(cache_saved, 16)

        @block.gpsimd
        def _(pool):
            nc.gpsimd.memset(ones[:], 1.0).then_inc(consts_made, 1)
            nc.gpsimd.memset(eps[:], EPS).then_inc(consts_made, 1)
            nc.gpsimd.iota(iota_i[:], [[1, P]], base=0, channel_multiplier=0).then_inc(iota_made, 1)
            nc.gpsimd.memset(ident[:], 0.0).then_inc(ident_made, 1)
            pool.wait_ge(ident_made, 1)
            nc.gpsimd.affine_select(out=ident[:], in_=ident[:], compare_op=ALU.not_equal, fill=1.0, base=0,
                                    pattern=[[-1, P]], channel_multiplier=1).then_inc(ident_made, 1)

            def split_low(lap, j):
                pool.wait_ge(raw_in[j], 16 * (lap + 1))
                pool.wait_ge(hi_made, RING * lap + j + 1)
                if not (isinstance(lap, int) and lap == 0):
                    pool.wait_ge(unit_done, RING * (lap - 1) + j + 1)
                nc.gpsimd.tensor_tensor(w_lo[:, j, :], raw[:, j, :], w_hi[:, j, :].bitcast(F32),
                                        ALU.subtract).then_inc(lo_made, 1)

            for j in range(RING):
                split_low(0, j)
            with pool.Fori(1, N_UNITS // RING) as lap:
                for j in range(RING):
                    split_low(lap, j)

        @block.tensor
        def _(pe):
            def unit(lap, j, hi, lo):
                u = RING * lap + j
                pe.wait_ge(hi_made, u + 1)
                pe.wait_ge(lo_made, u + 1)
                out = unit_psum(j)
                for k in range(KC):
                    for n, (w, m) in enumerate(((w_hi, hi), (w_hi, lo), (w_lo, hi))):
                        for a in range(2):
                            last = nc.tensor.matmul(out[:, a, :], w[:, j, k * P:(k + 1) * P],
                                                    m[:, k, a * HALF:(a + 1) * HALF],
                                                    start=(k == 0 and n == 0), stop=(k == KC - 1 and n == 2))
                last.then_inc(unit_done, 1)

            def channel_sum(src, chunks, to):
                for k in range(chunks):
                    for a in range(2):
                        last = nc.tensor.matmul(sum_psum(to)[:, a, :], ones[:], src(k)[:, a * HALF:(a + 1) * HALF],
                                                start=(k == 0), stop=(k == chunks - 1))
                last.then_inc(sum_done, 1)

            pe.wait_ge(consts_made, 2)
            pe.wait_ge(sq_made, KC)
            channel_sum(lambda k: sq[:, k], KC, 0)
            pe.wait_ge(mov_hi_made, KC)
            pe.wait_ge(mov_lo_made, KC)
            for j in range(RING):
                if j >= 2:
                    pe.wait_ge(act_took, j - 1)
                unit(0, j, mov_hi, mov_lo)
            with pe.Fori(1, N_IN // RING) as lap:
                for j in range(RING):
                    pe.wait_ge(act_took, RING * lap + j - 1)
                    unit(lap, j, mov_hi, mov_lo)
            pe.wait_ge(conv_b_made, WC)
            channel_sum(lambda c: proj[:, 2 * c], WC, 0)
            pe.wait_ge(sq_made, KC + WC)
            channel_sum(lambda c: sq[:, WC + c], WC, 1)
            pe.wait_ge(std_made, 2)
            pe.wait_ge(sq_made, KC + 2 * WC)
            channel_sum(lambda c: sq[:, c], WC, 1)
            pe.wait_ge(sq_made, KC + 3 * WC)
            channel_sum(lambda c: sq[:, c], WC, 0)
            pe.wait_ge(mov_hi_made, 2 * KC)
            pe.wait_ge(mov_lo_made, 2 * KC)
            pe.wait_ge(act_took, N_IN)
            for n in range(N_OUT):
                if n >= 2:
                    pe.wait_ge(dve_took, n - 1)
                unit(FIRST_OUT // RING + n // RING, n % RING, mov_hi, mov_lo)
            pe.wait_ge(sq_made, 2 * KC + 3 * WC)
            channel_sum(lambda k: sq[:, k], KC, 0)
            pe.wait_ge(mov_hi_made, 3 * KC)
            pe.wait_ge(mov_lo_made, 3 * KC)
            pe.wait_ge(dve_took, N_OUT)
            pe.wait_ge(keys_in, 16)

            def head_scores(head, s):
                pe.wait_ge(act_took, N_IN + 2 * head + 2)
                if not (isinstance(head, int) and head == 0):
                    pe.wait_ge(scores_took, head)
                for t in range(TILES):
                    n = min(P, T - t * P)
                    for side in range(2):
                        last = nc.tensor.matmul(ps_misc[0:n, t // 2, (t % 2) * 256 + side * P:(t % 2) * 256 + side * P + P],
                                                q_ring[:, 2 * s + side, t * P:t * P + n],
                                                key_view(head, s, side), start=True, stop=True)
                last.then_inc(scores_done, 1)

            def key_view(head, s, side):
                return keys[:, bass.ds(2 * head + side, 1), :].rearrange("p a n -> p (a n)")

            for n in range(RING):
                if n >= 2:
                    pe.wait_ge(act_took, N_IN + n - 1)
                unit(FIRST_Q // RING, n, mov_hi, mov_lo)
                if n == 2:
                    head_scores(0, 0)
            with pe.Fori(1, N_Q // RING) as lap:
                for j in range(RING):
                    pe.wait_ge(act_took, N_IN + RING * lap + j - 1)
                    unit(FIRST_Q // RING + lap, j, mov_hi, mov_lo)
                    if j == 0:
                        head_scores(2 * lap - 1, 1)
                    if j == 2:
                        head_scores(2 * lap, 0)

            def u_unit(lap, j):
                pe.wait_ge(act_took, N_IN + N_Q + RING * lap + j - 1)
                unit(FIRST_U // RING + lap, j, mov_hi, mov_lo)

            for j in range(RING):
                u_unit(0, j)
                if j == 0:
                    head_scores(HEADS - 1, 1)
            with pe.Fori(1, U_BEFORE) as lap:
                for j in range(RING):
                    u_unit(lap, j)
            pe.wait_ge(gate_made, 1)
            pe.wait_ge(ident_made, 2)
            pe.wait_ge(scores_took, HEADS)
            for n in range(3):
                if n == 2:
                    pe.wait_ge(turned_took, 1)
                for t in range(TILES):
                    src = ij[:, n, t] if n < 2 else gate[:, t * HEADS:(t + 1) * HEADS]
                    last = nc.tensor.transpose(ps_misc[:, 2 * (n % 2) + t // 4, (t % 4) * P:(t % 4 + 1) * P],
                                               src.rearrange("p h k -> p (h k)"), ident[:])
                last.then_inc(turned, 1)
            pe.wait_ge(turned_took, 3)

            def gate_batch(tg, b):
                n = BATCHES * tg + b
                pe.wait_ge(hot_made, n + 1)
                if not (isinstance(tg, int) and tg == 0 and b < 4):
                    pe.wait_ge(g_took, n - 3)
                for x in range(BATCH):
                    for m, g in enumerate((gated_hi, gated_lo)):
                        last = nc.tensor.matmul(ps_misc[:, b % 4, x * P:(x + 1) * P], hot_j[:, b % 2, x],
                                                g[:, b % 2, x], start=(m == 0), stop=(m == 1))
                last.then_inc(g_done, 1)

            def gate_group(tg):
                for j in range(RING):
                    gate_batch(tg, 2 * j)
                    gate_batch(tg, 2 * j + 1)
                    u_unit(tg + U_BEFORE, j)

            gate_group(0)
            with pe.Fori(1, GTS) as tg:
                gate_group(tg)
            with pe.Fori(N_U // RING - U_AFTER, N_U // RING) as lap:
                for j in range(RING):
                    u_unit(lap, j)

            def value_group(pair_lap, s):
                g = 2 * pair_lap + s
                pe.wait_ge(prod_made, GROUP * (g + 1))
                for n in range(KC):
                    first = isinstance(pair_lap, int) and pair_lap == 0 and s == 0 and n < 2
                    if not first:
                        pe.wait_ge(dve_took, N_OUT + KC * g + n - 1)
                    unit(FIRST_V // RING + 2 * g + n // RING, n % RING, prod_hi[:, s], prod_lo[:, s])

            pe.wait_ge(act_took, N_IN + N_Q + N_U)
            value_group(0, 0)
            value_group(0, 1)
            with pe.Fori(1, GROUPS // 2) as pair_lap:
                value_group(pair_lap, 0)
                value_group(pair_lap, 1)
            pe.wait_ge(sq_made, 3 * KC + 3 * WC)
            channel_sum(lambda k: sq_f[:, k], KC, 0)

        @block.scalar
        def _(act):
            def split_high(lap, j):
                lap, j = lap + j // RING, j % RING
                act.wait_ge(raw_in[j], 16 * (lap + 1))
                if not (isinstance(lap, int) and lap == 0):
                    act.wait_ge(unit_done, RING * (lap - 1) + j + 1)
                nc.scalar.activation(w_hi[:, j, :], raw[:, j, :], ACT.Copy).then_inc(hi_made, 1)

            def take(lap, j, out, func=ACT.Copy):
                act.wait_ge(unit_done, RING * lap + j + 1)
                nc.scalar.activation(halves(out), unit_psum(j), func).then_inc(act_took, 1)

            def root(n, to, scale):
                act.wait_ge(sum_done, n)
                nc.scalar.activation(halves(std[:]), sum_psum(to), ACT.Sqrt, bias=eps[:], scale=scale).then_inc(std_made, 1)

            def mov_high(n0, chunks):
                for n, k in enumerate(chunks):
                    act.wait_ge(nrm_made, n0 + n + 1)
                    nc.scalar.activation(mov_hi[:, k], nrm[:, k], ACT.Copy).then_inc(mov_hi_made, 1)

            act.wait_ge(x_in, 16)
            act.wait_ge(consts_made, 2)
            for k in range(KC):
                nc.scalar.activation(sq[:, k], hid[:, k], ACT.Square).then_inc(sq_made, 1)
            split_high(0, 0)
            split_high(0, 1)
            root(1, 0, 1.0 / D)
            mov_high(0, range(KC))

            def mix_unit(lap, j, func):
                split_high(lap, j + 2)
                out = proj[:, bass.ds(RING * lap + j, 1)].rearrange("p a t -> p (a t)")
                take(lap, j, out, func)

            for lap in range(2 * WC // RING):
                for j in range(RING):
                    mix_unit(lap, j, ACT.Sigmoid if j % 2 else ACT.Copy)
            with act.Fori(2 * WC // RING, N_IN // RING) as lap:
                for j in range(RING):
                    mix_unit(lap, j, ACT.Copy)
            for c in range(WC):
                act.wait_ge(ya_made, c + 1)
                nc.scalar.activation(sq[:, WC + c], proj[:, 2 * WC + 3 * c], ACT.Square).then_inc(sq_made, 1)
            root(3, 1, 1.0 / WIDTH)
            mov_high(KC, range(WC))
            act.wait_ge(cache_made, 1)
            act.dma_start(caches, cache_out[:]).then_inc(cache_saved, 16)
            for c in range(WC):
                act.wait_ge(centred, c + 1)
                nc.scalar.activation(sq[:, c], proj[:, 2 * c], ACT.Square).then_inc(sq_made, 1)
            root(4, 1, 1.0 / WIDTH)
            for c in range(WC):
                act.wait_ge(scaled_b, c + 1)
                nc.scalar.activation(proj[:, 2 * c + 1], proj[:, 2 * c], ACT.Silu, bias=par_col("conv_norm_b", c),
                                     scale=par_col("conv_norm_g", c)).then_inc(silu_made, 1)
            for c in range(WC):
                act.wait_ge(silu_made, c + 1)
                nc.scalar.activation(sq[:, c], proj[:, 2 * c + 1], ACT.Square).then_inc(sq_made, 1)
            root(5, 0, 1.0 / WIDTH)
            mov_high(KC + WC, range(WC, KC))
            for n in range(N_OUT):
                split_high(FIRST_OUT // RING, n + 2)
                act.wait_ge(dve_took, n + 1)
                nc.scalar.activation(sq[:, n], hid[:, n], ACT.Square).then_inc(sq_made, 1)
            root(6, 0, 1.0 / D)
            mov_high(2 * KC, range(KC))

            def take_scores(head):
                act.wait_ge(scores_done, head + 1)
                for b in range(2):
                    nc.scalar.activation(
                        scores[:, bass.ds(head, 1), 2 * b:2 * b + 2, :].rearrange("p a t n -> p (a t n)"),
                        ps_misc[:, b, :], ACT.Copy)
                nc.scalar.activation(
                    scores[0:T_SAMPLE, bass.ds(head, 1), TILES - 1, :].rearrange("p a n -> p (a n)"),
                    ps_misc[0:T_SAMPLE, 2, 0:2 * NKEYS], ACT.Copy).then_inc(scores_took, 1)

            def q_unit(lap, j):
                split_high(FIRST_Q // RING + lap, j + 2)
                take(FIRST_Q // RING + lap, j, q_ring[:, j])

            act.wait_ge(mov_lo_made, 3 * KC)
            act.dma_start(keys[:], sub_keys).then_inc(keys_in, 16)
            for j in range(RING):
                q_unit(0, j)
                if j == 2:
                    take_scores(0)
            with act.Fori(1, N_Q // RING) as lap:
                for j in range(RING):
                    q_unit(lap, j)
                    if j == 0:
                        take_scores(2 * lap - 1)
                    if j == 2:
                        take_scores(2 * lap)

            def spill(lap, j):
                act.wait_ge(act_took, N_IN + N_Q + RING * lap + j + 1)
                dst = acts_dram[bass.ds(RING * lap + j, 1)].rearrange("a p t -> p (a t)")
                act.dma_start(dst, act_ring[:, j % 2]).then_inc(act_saved[j], 16)

            def u_unit(lap, j, first=False, between=None):
                split_high(FIRST_U // RING + lap, j + 2)
                if not first:
                    act.wait_ge(act_saved[(j + 2) % RING], 16 * (lap + j // 2))
                if between:
                    between()
                take(FIRST_U // RING + lap, j, act_ring[:, j % 2], ACT.Gelu)
                spill(lap, j)

            for j in range(RING):
                u_unit(0, j, first=j < 2)
                if j == 0:
                    take_scores(HEADS - 1)
            with act.Fori(1, U_BEFORE) as lap:
                for j in range(RING):
                    u_unit(lap, j)
            act.wait_ge(shifted, 1)
            nc.scalar.activation(gate[:], gate[:], ACT.Exp).then_inc(exp_made, 1)
            for n, dst in enumerate((ij_t[:, 0], ij_t[:, 1], gate_t[:])):
                act.wait_ge(turned, n + 1)
                nc.scalar.activation(dst[:, 0:T_PROMPT], ps_misc[:, 2 * (n % 2), :], ACT.Copy)
                nc.scalar.activation(dst[:, T_PROMPT:T], ps_misc[:, 2 * (n % 2) + 1, 0:T_SAMPLE],
                                     ACT.Copy).then_inc(turned_took, 1)

            def take_gates(tg, s, b):
                act.wait_ge(g_done, BATCHES * tg + b + 1)
                nc.scalar.activation(gates[:, s, :, BATCH * b:BATCH * (b + 1)].rearrange("p i t -> p t i"),
                                     ps_misc[:, b % 4, :].rearrange("p (t i) -> p t i", t=BATCH),
                                     ACT.Copy).then_inc(g_took, 1)

            def gate_group(tg, s, first):
                for j in range(RING):
                    def between():
                        if j == 0 and not first:
                            act.wait_ge(g_saved[s], 8 * (tg - s))
                        take_gates(tg, s, 2 * j)
                        take_gates(tg, s, 2 * j + 1)
                    u_unit(U_BEFORE + tg, j, between=between)
                act.wait_ge(g_took, BATCHES * (tg + 1))
                dst = gates_dram[bass.ds(tg, 1)].rearrange("a p i t -> p (a i t)")
                act.dma_start(dst, gates[:, s].rearrange("p i t -> p (i t)")).then_inc(g_saved[s], 16)

            gate_group(0, 0, True)
            gate_group(1, 1, True)
            with act.Fori(1, GTS // 2) as pair_lap:
                gate_group(2 * pair_lap, 0, False)
                gate_group(2 * pair_lap + 1, 1, False)
            gate_group(GTS - 1, 0, False)
            with act.Fori(N_U // RING - U_AFTER, N_U // RING) as lap:
                for j in range(RING):
                    u_unit(lap, j)
            with act.Fori(FIRST_V // RING, N_UNITS // RING - 1) as lap:
                for j in range(RING):
                    split_high(lap, j + 2)
            for j in range(2):
                split_high(N_UNITS // RING - 1, j + 2)
            for n in range(KC):
                act.wait_ge(dve_took, N_OUT + N_V - KC + n + 1)
                nc.scalar.activation(sq_f[:, n], hid[:, n], ACT.Square).then_inc(sq_made, 1)
            root(7, 0, 1.0 / D)
            for k in range(KC):
                act.wait_ge(y_made, k + 1)
                act.dma_start(y_t[:, k, :], y_sb[:, k]).then_inc(y_saved, 16)

        @block.vector
        def _(dve):
            count = {"n": 0, "loop": 0}

            def step(ins):
                ins.then_inc(dve_step, 1)
                count["n"] += 1

            def settle():
                dve.wait_ge(dve_step, count["n"] + count["loop"])

            def settle_for_max():
                settle()
                dve.sem_inc(dve_step, 1)
                count["n"] += 1

            def norm_chunks(n_std, src, gains, chunks):
                dve.wait_ge(std_made, n_std)
                step(nc.vector.reciprocal(rstd[:], std[:]))
                settle()
                for k in chunks:
                    nc.vector.scalar_tensor_tensor(out=nrm[:, k], in0=src(k), scalar=gains(k), in1=rstd[:],
                                                   op0=ALU.mult, op1=ALU.mult).then_inc(nrm_made, 1)

            def mov_low(n0, chunks):
                for n, k in enumerate(chunks):
                    dve.wait_ge(mov_hi_made, n0 + n + 1)
                    dve.wait_ge(nrm_made, n0 + n + 1)
                    nc.vector.tensor_tensor(mov_lo[:, k], nrm[:, k], mov_hi[:, k].bitcast(F32),
                                            ALU.subtract).then_inc(mov_lo_made, 1)

            dve.wait_ge(params_in, 16)
            nc.vector.memset(pad_a[:, :, 0:HIST_A], 0.0)
            nc.vector.memset(pad_b[:, :, 0:HIST_B], 0.0)
            nc.vector.tensor_copy(pad_a[:, :, HIST_A + T_PROMPT:2 * HIST_A + T_PROMPT],
                                  par_col("hist_a", 0, WC * HIST_A).rearrange("p (c n) -> p c n", c=WC))
            step(nc.vector.tensor_copy(pad_b[:, :, HIST_B + T_PROMPT:2 * HIST_B + T_PROMPT],
                                       par_col("hist_b", 0, WC * HIST_B).rearrange("p (c n) -> p c n", c=WC)))
            dve.wait_ge(x_in, 16)
            norm_chunks(1, lambda k: hid[:, k], lambda k: par_col("mix_g", k), range(KC))
            mov_low(0, range(KC))

            def causal_conv(pad, hist, taps, weight, bias, out, c):
                n = hist + T
                acc = conv[:, 0:n]
                if bias is None:
                    step(nc.vector.tensor_scalar(acc, pad[:, c, 0:n], weight(0), None, ALU.mult))
                else:
                    step(nc.vector.tensor_scalar(acc, pad[:, c, 0:n], weight(0), bias, ALU.mult, ALU.add))
                settle()
                for k in range(1, taps - 1):
                    step(nc.vector.scalar_tensor_tensor(out=acc, in0=pad[:, c, k:k + n], scalar=weight(k), in1=acc,
                                                        op0=ALU.mult, op1=ALU.add))
                    settle()
                for at, to, m in ((0, 0, T_PROMPT), (T_PROMPT + hist, T_PROMPT, T_SAMPLE)):
                    last = nc.vector.scalar_tensor_tensor(
                        out=out[:, to:to + m], in0=pad[:, c, at + taps - 1:at + taps - 1 + m],
                        scalar=weight(taps - 1), in1=conv[:, at:at + m], op0=ALU.mult, op1=ALU.add)
                return last

            for c in range(WC):
                dve.wait_ge(act_took, 2 * c + 2)
                nc.vector.tensor_tensor(pad_b[:, c, HIST_B:HIST_B + T_PROMPT], proj[:, 2 * c, 0:T_PROMPT],
                                        proj[:, 2 * c + 1, 0:T_PROMPT], ALU.mult)
                step(nc.vector.tensor_tensor(pad_b[:, c, 2 * HIST_B + T_PROMPT:PAD_B], proj[:, 2 * c, T_PROMPT:T],
                                             proj[:, 2 * c + 1, T_PROMPT:T], ALU.mult))
                settle()
                causal_conv(pad_b, HIST_B, TAPS_B, lambda k: par_col("conv_b_w", c * TAPS_B + k), par_col("conv_b_b", c),
                            proj[:, 2 * c], c).then_inc(conv_b_made, 1)
            for c in range(WC):
                h, cc, b = (proj[:, 2 * WC + 3 * c + n] for n in range(3))
                dve.wait_ge(act_took, 2 * WC + 3 * c + 3)
                nc.vector.tensor_tensor(pad_a[:, c, HIST_A:HIST_A + T_PROMPT], h[:, 0:T_PROMPT], cc[:, 0:T_PROMPT], ALU.mult)
                step(nc.vector.tensor_tensor(pad_a[:, c, 2 * HIST_A + T_PROMPT:PAD_A], h[:, T_PROMPT:T],
                                             cc[:, T_PROMPT:T], ALU.mult))
                settle()
                step(causal_conv(pad_a, HIST_A, TAPS_A, lambda k: par_col("conv_a_w", c * TAPS_A + k), None, h, c))
                settle()
                nc.vector.tensor_tensor(h, h, b, ALU.mult).then_inc(ya_made, 1)
            for pad, hist, at in ((pad_a, HIST_A, 0), (pad_b, HIST_B, CACHE_A)):
                out = cache_out[:, at:at + WC * 2 * hist].rearrange("p (c s n) -> p c s n", c=WC, s=2)
                nc.vector.tensor_copy(out[:, :, 0, :], pad[:, :, T_PROMPT:T_PROMPT + hist])
                last = nc.vector.tensor_copy(out[:, :, 1, :], pad[:, :, 2 * hist + T - hist:2 * hist + T])
            last.then_inc(cache_made, 1)
            dve.wait_ge(sum_done, 2)
            mean = conv[:, 0:T]
            step(nc.vector.tensor_scalar(halves(mean), sum_psum(0), 1.0 / WIDTH, None, ALU.mult))
            settle()
            for c in range(WC):
                nc.vector.tensor_tensor(proj[:, 2 * c], proj[:, 2 * c], mean, ALU.subtract).then_inc(centred, 1)
            norm_chunks(2, lambda c: proj[:, 2 * WC + 3 * c], lambda c: par_col("out_a_g", c), range(WC))
            mov_low(KC, range(WC))
            dve.wait_ge(std_made, 3)
            step(nc.vector.reciprocal(rstd[:], std[:]))
            settle()
            dve.wait_ge(centred, WC)
            for c in range(WC):
                nc.vector.tensor_tensor(proj[:, 2 * c], proj[:, 2 * c], rstd[:], ALU.mult).then_inc(scaled_b, 1)
            dve.wait_ge(silu_made, WC)
            norm_chunks(4, lambda k: proj[:, 2 * (k - WC) + 1], lambda k: par_col("out_b_g", k - WC), range(WC, KC))
            mov_low(KC + WC, range(WC, KC))
            for n in range(N_OUT):
                dve.wait_ge(unit_done, FIRST_OUT + n + 1)
                nc.vector.tensor_tensor(halves(hid[:, n]), halves(hid[:, n]), unit_psum(n), ALU.add).then_inc(dve_took, 1)
            dve.wait_ge(dve_took, N_OUT)
            norm_chunks(5, lambda k: hid[:, k], lambda k: par_col("ffn_g", k), range(KC))
            mov_low(2 * KC, range(KC))

            dve.wait_ge(iota_made, 1)
            dve.wait_ge(mov_lo_made, 3 * KC)
            step(nc.vector.tensor_copy(iota[:], iota_i[:]))
            settle()
            step(nc.vector.memset(cur[:, TILES - 1], 0.0))
            settle()
            start = count["n"]
            LOWEST = -3.0e38
            with dve.Fori(0, HEADS) as head:
                PER_HEAD = 27
                count["loop"] = head * PER_HEAD
                dve.wait_ge(scores_took, head + 1)
                settle()
                rows = [(t, s) for t in range(TILES) for s in range(2)]

                for t0, t1, rows_in in ((0, TILES - 1, P), (TILES - 1, TILES, T_SAMPLE)):
                    last = nc.vector.tensor_copy(
                        cur[0:rows_in, t0:t1], scores[0:rows_in, bass.ds(head, 1), t0:t1].rearrange("p a t n -> p (a t) n"))
                step(last)
                settle_for_max()
                for t, s in rows:
                    last = nc.vector.max(best[:, t, s, 0:8], cur[:, t, s * NKEYS:(s + 1) * NKEYS])
                step(last)
                settle_for_max()
                for t, s in rows:
                    c = cur[:, t, s * NKEYS:(s + 1) * NKEYS]
                    nc.vector.max_index(best_at[:, t, s, 0:8], best[:, t, s, 0:8], c)
                    last = nc.vector.match_replace(cur[:, t, s * NKEYS:(s + 1) * NKEYS], best[:, t, s, 0:8], c, LOWEST)
                step(last)
                settle_for_max()
                for t, s in rows:
                    last = nc.vector.max(best[:, t, s, 8:16], cur[:, t, s * NKEYS:(s + 1) * NKEYS])
                step(last)
                settle_for_max()
                for t, s in rows:
                    last = nc.vector.max_index(best_at[:, t, s, 8:16], best[:, t, s, 8:16],
                                               cur[:, t, s * NKEYS:(s + 1) * NKEYS])
                step(last)
                shape = [P, TILES, TOPK, TOPK]
                step(nc.vector.tensor_tensor(pair[:], best[:, :, 0, :].unsqueeze(3).broadcast_to(shape),
                                             best[:, :, 1, :].unsqueeze(2).broadcast_to(shape), ALU.add))
                settle_for_max()
                tile_pairs = [pair[:, t].rearrange("p a b -> p (a b)") for t in range(TILES)]
                for t in range(TILES):
                    last = nc.vector.max(top[:, t, 0:8], tile_pairs[t])
                step(last)
                settle_for_max()
                for t in range(TILES):
                    nc.vector.max_index(pair_at[:, t, 0:8], top[:, t, 0:8], tile_pairs[t])
                    last = nc.vector.match_replace(tile_pairs[t], top[:, t, 0:8], tile_pairs[t], LOWEST)
                step(last)
                settle_for_max()
                for t in range(TILES):
                    last = nc.vector.max(top[:, t, 8:16], tile_pairs[t])
                step(last)
                settle_for_max()
                for t in range(TILES):
                    last = nc.vector.max_index(pair_at[:, t, 8:16], top[:, t, 8:16], tile_pairs[t])
                step(last)
                settle()
                spare = cur[:].rearrange("p t (a b) -> p t a b", b=TOPK)
                nc.vector.tensor_copy(tops[:].rearrange("p (t h) k -> p t h k", h=HEADS)[:, :, bass.ds(head, 1), :]
                                      .rearrange("p t a k -> p t (a k)"), top[:])
                nc.vector.tensor_scalar(rank_u[:, 0], pair_at[:], 4, None, ALU.logical_shift_right)
                nc.vector.tensor_scalar(rank_u[:, 1], pair_at[:], TOPK - 1, None, ALU.bitwise_and)
                step(nc.vector.tensor_copy(best_at_f[:], best_at[:]))
                settle()
                step(nc.vector.tensor_copy(rank[:], rank_u[:]))
                settle()
                for s, buf in ((0, pair[:]), (1, spare)):
                    last = nc.vector.tensor_tensor(buf, rank[:, s].unsqueeze(3).broadcast_to(shape),
                                                   iota[:, 0:TOPK].unsqueeze(1).unsqueeze(1).broadcast_to(shape),
                                                   ALU.is_equal)
                step(last)
                settle()
                for s, buf in ((0, pair[:]), (1, spare)):
                    last = nc.vector.tensor_tensor(buf, buf, best_at_f[:, :, s].unsqueeze(2).broadcast_to(shape),
                                                   ALU.mult)
                step(last)
                settle()
                for s, buf in ((0, pair[:]), (1, spare)):
                    last = nc.vector.tensor_reduce(
                        ij[:, s, :, bass.ds(head, 1), :].rearrange("p t a k -> p t (a k)"), buf, AX_X, ALU.add)
                step(last)
                settle()
                while count["n"] - start < PER_HEAD:
                    dve.sem_inc(dve_step, 1)
                    count["n"] += 1
                assert count["n"] - start == PER_HEAD, count["n"] - start
            count["n"] = start + HEADS * PER_HEAD
            count["loop"] = 0
            settle()
            rows = [P, TILES * HEADS, TOPK]
            nc.vector.tensor_tensor(gate[:], tops[:], tops[:, :, 0:1].broadcast_to(rows),
                                    ALU.subtract).then_inc(shifted, 1)
            dve.wait_ge(exp_made, 1)
            step(nc.vector.tensor_reduce(gate_sum[:], gate[:], AX_X, ALU.add))
            settle()
            step(nc.vector.reciprocal(gate_sum[:], gate_sum[:]))
            settle()
            nc.vector.tensor_tensor(gate[:], gate[:], gate_sum[:].unsqueeze(2).broadcast_to(rows),
                                    ALU.mult).then_inc(gate_made, 1)
            dve.wait_ge(turned_took, 3)
            step(nc.vector.tensor_copy(gate_hi[:], gate_t[:]))
            settle()
            step(nc.vector.tensor_tensor(gate_lo[:], gate_t[:], gate_hi[:].bitcast(F32), ALU.subtract))
            settle()

            hots = [P, BATCH, P]

            def hot_batch(tg, b):
                n, s = BATCHES * tg + b, b % 2
                if not (isinstance(tg, int) and tg == 0 and b < 2):
                    dve.wait_ge(g_done, n - 1)
                at = bass.ds(BATCH * n, BATCH)
                keys_of = iota[:].unsqueeze(1).broadcast_to(hots)
                nc.vector.tensor_tensor(hot_i[:, s], ij_t[:, 0, at].unsqueeze(2).broadcast_to(hots), keys_of,
                                        ALU.is_equal).then_inc(dve_step, 1)
                nc.vector.tensor_tensor(hot_j[:, s], ij_t[:, 1, at].unsqueeze(2).broadcast_to(hots), keys_of,
                                        ALU.is_equal)
                dve.wait_ge(dve_step, hot_start + n + 1)
                nc.vector.tensor_tensor(gated_hi[:, s], hot_i[:, s], gate_hi[:, at].bitcast(F32).unsqueeze(2).broadcast_to(hots),
                                        ALU.mult)
                nc.vector.tensor_tensor(gated_lo[:, s], hot_i[:, s], gate_lo[:, at].unsqueeze(2).broadcast_to(hots),
                                        ALU.mult).then_inc(hot_made, 1)

            hot_start = count["n"]
            for b in range(BATCHES):
                hot_batch(0, b)
            with dve.Fori(1, GTS) as tg:
                for b in range(BATCHES):
                    hot_batch(tg, b)
            count["n"] += GTS * BATCHES

            prod_start = count["n"]

            def product(pair_lap, s, e):
                g = 2 * pair_lap + s
                n = GROUP * g + e
                half, x = e // 4, e % 4
                if x == 0:
                    dve.wait_ge(gates_back[half], 16 * (g + 1))
                if x % 2 == 0:
                    dve.wait_ge(acts_back[x // 2], 16 * (2 * g + half + 1))
                if not (isinstance(n, int) and n == 0):
                    dve.wait_ge(prod_made, n)
                p = prod[:]
                nc.vector.tensor_tensor(p.rearrange("p (g t) -> p g t", g=GTS),
                                        acts_in[:, x // 2, x % 2].rearrange("p (g t) -> p g t", g=GTS),
                                        gates_in[:, half, :, x, :], ALU.mult).then_inc(dve_step, 1)
                dve.wait_ge(dve_step, prod_start + 2 * n + 1)
                nc.vector.tensor_copy(prod_hi[:, s, e], p).then_inc(dve_step, 1)
                dve.wait_ge(dve_step, prod_start + 2 * n + 2)
                nc.vector.tensor_tensor(prod_lo[:, s, e], p, prod_hi[:, s, e].bitcast(F32),
                                        ALU.subtract).then_inc(prod_made, 1)

            def collect(pair_lap, s, n):
                g = 2 * pair_lap + s
                dve.wait_ge(unit_done, FIRST_V + KC * g + n + 1)
                nc.vector.tensor_tensor(halves(hid[:, n]), halves(hid[:, n]), unit_psum(n), ALU.add).then_inc(dve_took, 1)

            for e in range(GROUP):
                product(0, 0, e)
            with dve.Fori(0, GROUPS // 2 - 1) as pair_lap:
                for s in range(2):
                    for n in range(KC):
                        product(pair_lap + s, 1 - s, n)
                        collect(pair_lap, s, n)
            for n in range(KC):
                product(GROUPS // 2 - 1, 1, n)
                collect(GROUPS // 2 - 1, 0, n)
            for n in range(KC):
                collect(GROUPS // 2 - 1, 1, n)
            count["n"] += 2 * N_U

            dve.wait_ge(dve_took, N_OUT + N_V)
            dve.wait_ge(std_made, 6)
            step(nc.vector.reciprocal(rstd[:], std[:]))
            settle()
            for k in range(KC):
                nc.vector.scalar_tensor_tensor(out=y_sb[:, k], in0=hid[:, k], scalar=par_col("final_g", k), in1=rstd[:],
                                               op0=ALU.mult, op1=ALU.mult).then_inc(y_made, 1)


def kernel(x_prompt, x_sample, cache_conv_a, cache_conv_b, norm_mix_g, w_in, conv_a_w, conv_b_w, conv_b_b,
           conv_norm_g, conv_norm_b, out_norm_a_g, out_norm_b_g, w_out, norm_ffn_g, w_q, sub_keys, u_experts,
           v_experts, final_norm_g):
    import numpy as np
    import concourse.bacc as bacc
    from concourse.bass_utils import run_bass_kernel_spmd

    def columns(w):
        w = np.asarray(w).reshape(KC, P, -1, P)
        return w.transpose(2, 1, 0, 3).reshape(-1, P, KC * P)

    def per_channel(a, chunks):
        a = np.asarray(a).reshape(chunks, P, -1)
        return a.transpose(1, 0, 2).reshape(P, -1)

    w_in_units = columns(w_in[0])
    order = [n * WC + c for c in range(WC) for n in (3, 4)] + [n * WC + c for c in range(WC) for n in (0, 1, 2)]
    u = np.asarray(u_experts[0]).reshape(NKEYS, P, KC, P).transpose(0, 3, 2, 1).reshape(N_U, P, KC * P)
    v = np.asarray(v_experts[0]).reshape(GROUPS, GROUP, P, KC, P).transpose(0, 3, 2, 1, 4).reshape(N_V, P, GROUP * P)
    stream = np.concatenate([w_in_units[order], columns(w_out[0]), columns(w_q[0]), u, v])
    x = np.concatenate([np.asarray(x_prompt[0]), np.asarray(x_sample[0])])
    x_t = np.ascontiguousarray(x.reshape(T, KC, P).transpose(2, 1, 0))
    params = np.concatenate([
        per_channel(norm_mix_g[0], KC), per_channel(norm_ffn_g[0], KC), per_channel(final_norm_g, KC),
        per_channel(np.asarray(conv_a_w[0]).T, WC), per_channel(np.asarray(conv_b_w[0]).T, WC),
        per_channel(conv_b_b[0], WC), per_channel(conv_norm_g[0], WC), per_channel(conv_norm_b[0], WC),
        per_channel(out_norm_a_g[0], WC), per_channel(out_norm_b_g[0], WC),
        per_channel(np.asarray(cache_conv_a[0, 0]).T, WC), per_channel(np.asarray(cache_conv_b[0, 0]).T, WC)], axis=1)
    keys = np.ascontiguousarray(np.asarray(sub_keys[0]).transpose(3, 0, 1, 2).reshape(P, 2 * HEADS, NKEYS))
    arrays = {"stream": stream, "x_t": x_t, "params": np.ascontiguousarray(params), "sub_keys": keys}

    nc = bacc.Bacc("TRN2", target_bir_lowering=False, num_devices=1)
    ins = [nc.dram_tensor(name, a.shape, mybir.dt.from_np(a.dtype), kind="ExternalInput").ap()
           for name, a in arrays.items()]
    y_t = nc.dram_tensor("y_t", (P, KC, T), F32, kind="ExternalOutput").ap()
    caches = nc.dram_tensor("caches", (P, N_CACHE), F32, kind="ExternalOutput").ap()
    build(nc, *ins, y_t, caches)
    got = run_bass_kernel_spmd(nc, [arrays], core_ids=[0]).results[0]
    y = got["y_t"].transpose(2, 1, 0).reshape(T, D)

    def cache(at, hist, which):
        c = got["caches"][:, at:at + WC * 2 * hist].reshape(P, WC, 2, hist)[:, :, which]
        return np.ascontiguousarray(c.transpose(2, 1, 0).reshape(1, 1, hist, WIDTH))

    return (np.ascontiguousarray(y[:T_PROMPT])[None], np.ascontiguousarray(y[T_PROMPT:])[None],
            cache(0, HIST_A, 0), cache(CACHE_A, HIST_B, 0), cache(0, HIST_A, 1), cache(CACHE_A, HIST_B, 1))
```

```python
from contextlib import ExitStack

import concourse.bass as bass
from concourse import mybir

F32 = mybir.dt.float32
F32R = mybir.dt.float32r
U32 = mybir.dt.uint32
I32 = mybir.dt.int32
F16 = mybir.dt.float16
ALU = mybir.AluOpType
ACT = mybir.ActivationFunctionType
AX_X = mybir.AxisListType.X

P = 128
D = 1024
KC = D // P
T_PROMPT, T_SAMPLE = 512, 32
T = T_PROMPT + T_SAMPLE
HALF = T // 2
WIDTH = 512
WC = WIDTH // P
TAPS_A, TAPS_B = 3, 31
HIST_A, HIST_B = TAPS_A - 1, TAPS_B - 1
PAD_A = 2 * HIST_A + T
PAD_B = 2 * HIST_B + T
HEADS, TOPK, NKEYS = 8, 16, 128
TILES = (T + P - 1) // P
EPS = 1e-6
XQ = 4

RING = 4
N_IN, N_OUT, N_Q = 5 * WC, KC, 2 * HEADS
N_U = NKEYS
GROUP = 8
GROUPS = NKEYS // GROUP
N_V = GROUPS * KC
OUTPUTS = 2 * KC
FIRST_OUT = N_IN
FIRST_Q = FIRST_OUT + N_OUT
FIRST_U = FIRST_Q + N_Q
FIRST_V = FIRST_U + N_U
N_UNITS = FIRST_V + N_V

GATE_UP = 2.0 ** 14
GT = 32
GTS = T // GT
BATCH = 4
BATCHES = GT // BATCH
U_BEFORE = 11
U_AFTER = N_U // RING - U_BEFORE - GTS

PARAMS = {}
N_PARAMS = 0
for _name, _n in (("mix_g", KC), ("ffn_g", KC), ("final_g", KC), ("conv_a_w", WC * TAPS_A),
                  ("conv_b_w", WC * TAPS_B), ("conv_b_b", WC), ("conv_norm_g", WC), ("conv_norm_b", WC),
                  ("out_a_g", WC), ("out_b_g", WC), ("hist_a", WC * HIST_A), ("hist_b", WC * HIST_B)):
    PARAMS[_name] = N_PARAMS
    N_PARAMS += _n
CACHE_A = WC * 2 * HIST_A
N_CACHE = CACHE_A + WC * 2 * HIST_B


def build(nc, stream, x_t, params, sub_keys, y_t, caches):
    gates_dram = nc.dram_tensor("gates_dram", (GTS, P, NKEYS, GT), F32, kind="Internal").ap()
    acts_dram = nc.dram_tensor("acts_dram", (N_U, P, T), F32, kind="Internal").ap()

    with ExitStack() as ctx:
        def sb_in(stack, name, shape, dt=F32):
            return stack.enter_context(nc.sbuf_tensor(name, shape, dt))

        def sb(name, shape, dt=F32):
            return sb_in(ctx, name, shape, dt)

        def sem(name):
            return ctx.enter_context(nc.semaphore(name))

        par = sb("par", [P, N_PARAMS])
        hid = sb("hid", [P, KC, T])
        mov_hi = sb("mov_hi", [P, KC, T], F32R)
        mov_lo = sb("mov_lo", [P, KC, T], F32R)
        raw = sb("raw", [P, RING, KC * P])
        w_hi = sb("w_hi", [P, RING, KC * P], F32R)
        w_lo = sb("w_lo", [P, RING, KC * P], F32R)
        ones = sb("ones", [P, P])
        eps = sb("eps", [P, 1])
        iota_i = sb("iota_i", [P, P], I32)
        iota = sb("iota", [P, P])
        ident = sb("ident", [P, P])
        std = sb("std", [P, T])
        rstd = sb("rstd", [P, T])
        cache_out = sb("cache_out", [P, N_CACHE])

        mixer = ExitStack()
        proj = sb_in(mixer, "proj", [P, N_IN, T])
        pad_a = sb_in(mixer, "pad_a", [P, WC, PAD_A])
        pad_b = sb_in(mixer, "pad_b", [P, WC, PAD_B])
        conv = sb_in(mixer, "conv", [P, PAD_B])
        nrm = sb_in(mixer, "nrm", [P, KC, T])
        sq = sb_in(mixer, "sq", [P, KC, T])
        mixer.close()

        act_ring = sb("act_ring", [P, 2, T])
        route = ExitStack()
        keys = sb_in(route, "keys", [P, 2 * HEADS, NKEYS])
        ij = sb_in(route, "ij", [P, 2, TILES, HEADS, TOPK])
        tops = sb_in(route, "tops", [P, TILES * HEADS, TOPK])
        gate = sb_in(route, "gate", [P, TILES * HEADS, TOPK])
        gate_sum = sb_in(route, "gate_sum", [P, TILES * HEADS])
        ij_t = sb_in(route, "ij_t", [P, 2, T])
        gate_t = sb_in(route, "gate_t", [P, T])
        gate_hi = sb_in(route, "gate_hi", [P, T], F16)
        gate_lo = sb_in(route, "gate_lo", [P, T])
        topk = ExitStack()
        scores = sb_in(topk, "scores", [P, HEADS, TILES, 2 * NKEYS])
        q_ring = sb_in(topk, "q_ring", [P, RING, T])
        cur = sb_in(topk, "cur", [P, TILES, 2 * NKEYS])
        best = sb_in(topk, "best", [P, TILES, 2, TOPK])
        best_at = sb_in(topk, "best_at", [P, TILES, 2, TOPK], U32)
        best_at_f = sb_in(topk, "best_at_f", [P, TILES, 2, TOPK])
        top = sb_in(topk, "top", [P, TILES, TOPK])
        pair = sb_in(topk, "pair", [P, TILES, TOPK, TOPK])
        pair_at = sb_in(topk, "pair_at", [P, TILES, TOPK], U32)
        rank_u = sb_in(topk, "rank_u", [P, 2, TILES, TOPK], U32)
        rank = sb_in(topk, "rank", [P, 2, TILES, TOPK])
        topk.close()
        build_g = ExitStack()
        gates = sb_in(build_g, "gates", [P, 2, NKEYS, GT])
        hot_j = sb_in(build_g, "hot_j", [P, 2, BATCH, P], F16)
        hot_i = sb_in(build_g, "hot_i", [P, 2, BATCH, P])
        gated_hi = sb_in(build_g, "gated_hi", [P, 2, BATCH, P], F16)
        gated_lo = sb_in(build_g, "gated_lo", [P, 2, BATCH, P], F16)
        build_g.close()
        route.close()

        values = ExitStack()
        acts_in = sb_in(values, "acts_in", [P, 2, 2, T])
        gates_in = sb_in(values, "gates_in", [P, 2, GTS, GROUP // 2, GT])
        prod = sb_in(values, "prod", [P, T])
        prod_hi = sb_in(values, "prod_hi", [P, 2, GROUP, T], F32R)
        prod_lo = sb_in(values, "prod_lo", [P, 2, GROUP, T], F32R)
        values.close()

        final = ExitStack()
        sq_f = sb_in(final, "sq_f", [P, KC, T])
        y_sb = sb_in(final, "y_sb", [P, KC, T])
        final.close()

        ps_unit = ctx.enter_context(nc.psum_tensor("ps_unit", [P, 4, 512], F32))
        ps_misc = ctx.enter_context(nc.psum_tensor("ps_misc", [P, 4, 512], F32))

        params_in = sem("params_in")
        x_in = [sem(f"x_in{q}") for q in range(XQ)]
        keys_in = sem("keys_in")
        raw_in = [sem(f"raw_in{s}") for s in range(RING)]
        hi_made = sem("hi_made")
        lo_made = sem("lo_made")
        unit_done = sem("unit_done")
        act_took = sem("act_took")
        dve_took = sem("dve_took")
        consts_made = sem("consts_made")
        iota_made = sem("iota_made")
        ident_made = sem("ident_made")
        sq_made = sem("sq_made")
        out_half_done = sem("out_half_done")
        hid_made = sem("hid_made")
        sum_done = sem("sum_done")
        std_made = sem("std_made")
        rstd_made = sem("rstd_made")
        nrm_made = sem("nrm_made")
        mov_hi_made = sem("mov_hi_made")
        mov_lo_made = sem("mov_lo_made")
        conv_b_made = sem("conv_b_made")
        ya_made = sem("ya_made")
        centred = sem("centred")
        scaled_b = sem("scaled_b")
        silu_made = sem("silu_made")
        cache_made = sem("cache_made")
        cache_saved = sem("cache_saved")
        scores_done = sem("scores_done")
        scores_took = sem("scores_took")
        shifted = sem("shifted")
        exp_made = sem("exp_made")
        gate_made = sem("gate_made")
        turned = sem("turned")
        turned_took = sem("turned_took")
        hot_made = sem("hot_made")
        g_done = sem("g_done")
        g_took = sem("g_took")
        g_saved = [sem(f"g_saved{s}") for s in range(2)]
        act_saved = [sem(f"act_saved{s}") for s in range(RING)]
        acts_back = [sem(f"acts_back{s}") for s in range(2)]
        gates_back = [sem(f"gates_back{s}") for s in range(2)]
        prod_made = sem("prod_made")
        dve_step = sem("dve_step")
        y_made = sem("y_made")
        y_saved = sem("y_saved")

        block = ctx.enter_context(nc.Block())

        def par_col(name, i, n=1):
            return par[:, PARAMS[name] + i:PARAMS[name] + i + n]

        def halves(ap):
            return ap.rearrange("p (a b) -> p a b", a=2)

        def unit_psum(j):
            return ps_unit[:, 2 * (j % 2):2 * (j % 2) + 2, 0:HALF]

        def sum_psum(pair_of_banks):
            return ps_misc[:, 2 * pair_of_banks:2 * pair_of_banks + 2, 0:HALF]


        @block.sync
        def _(sp):
            def load(lap, j):
                if not (isinstance(lap, int) and lap == 0):
                    sp.wait_ge(hi_made, RING * (lap - 1) + j + 1)
                    sp.wait_ge(lo_made, RING * (lap - 1) + j + 1)
                src = stream[bass.ds(RING * lap + j, 1)].rearrange("a p n -> p (a n)")
                sp.dma_start(raw[:, j, :], src).then_inc(raw_in[j], 16)

            def load_acts(half, q):
                for n in (2 * q, 2 * q + 1):
                    sp.wait_ge(act_saved[n], 16 * (half + 1))
                acts = acts_dram[bass.ds(4 * half + 2 * q, 2)].rearrange("e p t -> p e t")
                sp.dma_start(acts_in[:, q], acts).then_inc(acts_back[q], 16)

            def load_gates(pair_lap, s):
                g = gates_dram[:, :, bass.ds(4 * (2 * pair_lap + s), 4), :].rearrange("g p e t -> p g (e t)")
                sp.dma_start(gates_in[:, s].rearrange("p g e t -> p g (e t)"), g).then_inc(gates_back[s], 16)

            for q in range(XQ):
                part = slice(q * KC // XQ, (q + 1) * KC // XQ)
                sp.dma_start(hid[:, part], x_t[:, part]).then_inc(x_in[q], 16)
                if q == 0:
                    sp.dma_start(par[:], params).then_inc(params_in, 16)
            for j in range(RING):
                load(0, j)
            with sp.Fori(1, FIRST_V // RING - U_AFTER + 1) as lap:
                for j in range(RING):
                    load(lap, j)
            sp.wait_ge(g_saved[0], 16 * ((GTS + 1) // 2))
            sp.wait_ge(g_saved[1], 16 * (GTS // 2))
            for s in range(2):
                load_gates(0, s)
                load_acts(0, s)
            with sp.Fori(FIRST_V // RING - U_AFTER + 1, FIRST_V // RING) as lap:
                for j in range(RING):
                    load(lap, j)
            sp.wait_ge(prod_made, 2)
            load_acts(1, 0)

            def value_lap(pair_lap, s, gates_too=True):
                v = 8 * pair_lap + 4 * s
                sp.wait_ge(prod_made, v + 4)
                if gates_too:
                    load_gates(pair_lap + 1, s)
                load_acts(2 * pair_lap + s + 1, 1)
                for j in range(RING):
                    if j == 2 and gates_too:
                        sp.wait_ge(prod_made, v + 6)
                        load_acts(2 * pair_lap + s + 2, 0)
                    load(2 * pair_lap + s + FIRST_V // RING, j)

            with sp.Fori(0, GROUPS - 1) as pair_lap:
                value_lap(pair_lap, 0)
                value_lap(pair_lap, 1)
            value_lap(GROUPS - 1, 0, gates_too=False)
            for j in range(RING):
                load(N_UNITS // RING - 1, j)
            sp.wait_ge(y_saved, 16 * KC)
            sp.wait_ge(cache_saved, 16)

        @block.gpsimd
        def _(pool):
            nc.gpsimd.memset(ones[:], 1.0).then_inc(consts_made, 1)
            nc.gpsimd.memset(eps[:], EPS).then_inc(consts_made, 1)
            nc.gpsimd.iota(iota_i[:], [[1, P]], base=0, channel_multiplier=0).then_inc(iota_made, 1)
            nc.gpsimd.memset(ident[:], 0.0).then_inc(ident_made, 1)
            pool.wait_ge(ident_made, 1)
            nc.gpsimd.affine_select(out=ident[:], in_=ident[:], compare_op=ALU.not_equal, fill=1.0, base=0,
                                    pattern=[[-1, P]], channel_multiplier=1).then_inc(ident_made, 1)

            def split_low(lap, j):
                pool.wait_ge(raw_in[j], 16 * (lap + 1))
                pool.wait_ge(hi_made, RING * lap + j + 1)
                if not (isinstance(lap, int) and lap == 0):
                    pool.wait_ge(unit_done, RING * (lap - 1) + j + 1)
                nc.gpsimd.tensor_tensor(w_lo[:, j, :], raw[:, j, :], w_hi[:, j, :].bitcast(F32),
                                        ALU.subtract).then_inc(lo_made, 1)

            for j in range(RING):
                split_low(0, j)
            with pool.Fori(1, N_UNITS // RING) as lap:
                for j in range(RING):
                    split_low(lap, j)

        @block.tensor
        def _(pe):
            def unit(lap, j, hi, lo):
                u = RING * lap + j
                pe.wait_ge(hi_made, u + 1)
                pe.wait_ge(lo_made, u + 1)
                out = unit_psum(j)
                for k in range(KC):
                    for n, (w, m) in enumerate(((w_hi, hi), (w_hi, lo), (w_lo, hi))):
                        for a in range(2):
                            last = nc.tensor.matmul(out[:, a, :], w[:, j, k * P:(k + 1) * P],
                                                    m[:, k, a * HALF:(a + 1) * HALF],
                                                    start=(k == 0 and n == 0), stop=(k == KC - 1 and n == 2))
                last.then_inc(unit_done, 1)

            def channel_sum(src, ks, chunks, to, n_sq=None):
                for k in ks:
                    if n_sq is not None:
                        pe.wait_ge(sq_made, n_sq + k + 1)
                    for a in range(2):
                        last = nc.tensor.matmul(sum_psum(to)[:, a, :], ones[:], src(k)[:, a * HALF:(a + 1) * HALF],
                                                start=(k == 0), stop=(k == chunks - 1))
                    if k == chunks - 1:
                        last.then_inc(sum_done, 1)

            pe.wait_ge(consts_made, 2)
            channel_sum(lambda k: sq[:, k], range(KC), KC, 0, 0)
            pe.wait_ge(mov_hi_made, KC)
            pe.wait_ge(mov_lo_made, KC)
            for j in range(RING):
                if j >= 2:
                    pe.wait_ge(act_took, j - 1)
                unit(0, j, mov_hi, mov_lo)
            with pe.Fori(1, N_IN // RING) as lap:
                for j in range(RING):
                    pe.wait_ge(act_took, RING * lap + j - 1)
                    unit(lap, j, mov_hi, mov_lo)
            def out_unit(group, n):
                j = n % RING
                u = FIRST_OUT + group * WC + n
                pe.wait_ge(hi_made, u + 1)
                pe.wait_ge(lo_made, u + 1)
                for o in range(2):
                    q = KC * group + 2 * n + o
                    if q >= 2:
                        pe.wait_ge(dve_took, q - 1)
                    out = unit_psum(o)
                    for k in range(WC):
                        for m, (w, mov) in enumerate(((w_hi, mov_hi), (w_hi, mov_lo), (w_lo, mov_hi))):
                            for a in range(2):
                                at = (WC * o + k) * P
                                last = nc.tensor.matmul(out[:, a, :], w[:, j, at:at + P],
                                                        mov[:, WC * group + k, a * HALF:(a + 1) * HALF],
                                                        start=(k == 0 and m == 0), stop=(k == WC - 1 and m == 2))
                    last.then_inc(unit_done if o else out_half_done, 1)

            pe.wait_ge(conv_b_made, WC)
            channel_sum(lambda c: proj[:, 2 * c], range(WC), WC, 0)
            channel_sum(lambda c: sq[:, WC + c], range(WC), WC, 1, KC)
            pe.wait_ge(mov_hi_made, KC + WC)
            pe.wait_ge(mov_lo_made, KC + WC)
            pe.wait_ge(act_took, N_IN)
            out_unit(0, 0)
            out_unit(0, 1)
            pe.wait_ge(centred, WC)
            channel_sum(lambda c: sq[:, c], range(WC), WC, 0, KC + WC)
            out_unit(0, 2)
            out_unit(0, 3)
            pe.wait_ge(std_made, 2)
            channel_sum(lambda c: sq[:, c], range(WC), WC, 1, KC + 2 * WC)
            pe.wait_ge(mov_hi_made, 2 * KC)
            pe.wait_ge(mov_lo_made, 2 * KC)
            for n in range(WC):
                out_unit(1, n)
                if n > 0:
                    channel_sum(lambda k: sq[:, k], range(2 * n - 2, 2 * n), KC, 0, KC + 3 * WC)
            channel_sum(lambda k: sq[:, k], range(KC - 2, KC), KC, 0, KC + 3 * WC)
            pe.wait_ge(mov_hi_made, 3 * KC)
            pe.wait_ge(mov_lo_made, 3 * KC)
            pe.wait_ge(dve_took, OUTPUTS)
            pe.wait_ge(keys_in, 16)

            def head_scores(head, s):
                pe.wait_ge(act_took, N_IN + 2 * head + 2)
                if not (isinstance(head, int) and head == 0):
                    pe.wait_ge(scores_took, head)
                for t in range(TILES):
                    n = min(P, T - t * P)
                    for side in range(2):
                        last = nc.tensor.matmul(ps_misc[0:n, t // 2, (t % 2) * 256 + side * P:(t % 2) * 256 + side * P + P],
                                                q_ring[:, 2 * s + side, t * P:t * P + n],
                                                key_view(head, s, side), start=True, stop=True)
                last.then_inc(scores_done, 1)

            def key_view(head, s, side):
                return keys[:, bass.ds(2 * head + side, 1), :].rearrange("p a n -> p (a n)")

            for n in range(RING):
                if n >= 2:
                    pe.wait_ge(act_took, N_IN + n - 1)
                unit(FIRST_Q // RING, n, mov_hi, mov_lo)
                if n == 2:
                    head_scores(0, 0)
            with pe.Fori(1, N_Q // RING) as lap:
                for j in range(RING):
                    pe.wait_ge(act_took, N_IN + RING * lap + j - 1)
                    unit(FIRST_Q // RING + lap, j, mov_hi, mov_lo)
                    if j == 0:
                        head_scores(2 * lap - 1, 1)
                    if j == 2:
                        head_scores(2 * lap, 0)

            def u_unit(lap, j):
                pe.wait_ge(act_took, N_IN + N_Q + RING * lap + j - 1)
                unit(FIRST_U // RING + lap, j, mov_hi, mov_lo)

            for j in range(RING):
                u_unit(0, j)
                if j == 0:
                    head_scores(HEADS - 1, 1)
            with pe.Fori(1, U_BEFORE) as lap:
                for j in range(RING):
                    u_unit(lap, j)
            pe.wait_ge(gate_made, 1)
            pe.wait_ge(ident_made, 2)
            pe.wait_ge(scores_took, HEADS)
            for n in range(3):
                if n == 2:
                    pe.wait_ge(turned_took, 1)
                for t in range(TILES):
                    src = ij[:, n, t] if n < 2 else gate[:, t * HEADS:(t + 1) * HEADS]
                    last = nc.tensor.transpose(ps_misc[:, 2 * (n % 2) + t // 4, (t % 4) * P:(t % 4 + 1) * P],
                                               src.rearrange("p h k -> p (h k)"), ident[:])
                last.then_inc(turned, 1)
            pe.wait_ge(turned_took, 3)

            def gate_batch(tg, b):
                n = BATCHES * tg + b
                pe.wait_ge(hot_made, n + 1)
                if not (isinstance(tg, int) and tg == 0 and b < 4):
                    pe.wait_ge(g_took, n - 3)
                for x in range(BATCH):
                    for m, g in enumerate((gated_hi, gated_lo)):
                        last = nc.tensor.matmul(ps_misc[:, b % 4, x * P:(x + 1) * P], hot_j[:, b % 2, x],
                                                g[:, b % 2, x], start=(m == 0), stop=(m == 1))
                last.then_inc(g_done, 1)

            def gate_group(tg):
                for j in range(RING):
                    gate_batch(tg, 2 * j)
                    gate_batch(tg, 2 * j + 1)
                    u_unit(tg + U_BEFORE, j)

            gate_group(0)
            with pe.Fori(1, GTS) as tg:
                gate_group(tg)
            with pe.Fori(N_U // RING - U_AFTER, N_U // RING) as lap:
                for j in range(RING):
                    u_unit(lap, j)

            def value_group(pair_lap, s, final=False):
                g = 2 * pair_lap + s
                pe.wait_ge(prod_made, GROUP * (g + 1))
                for n in range(KC):
                    first = isinstance(pair_lap, int) and pair_lap == 0 and s == 0 and n < 2
                    if not first:
                        pe.wait_ge(dve_took, OUTPUTS + KC * g + n - 1)
                    unit(FIRST_V // RING + 2 * g + n // RING, n % RING, prod_hi[:, s], prod_lo[:, s])
                    if final and n >= 2:
                        channel_sum(lambda k: sq_f[:, k], (n - 2,), KC, 0, 2 * KC + 3 * WC)

            pe.wait_ge(act_took, N_IN + N_Q + N_U)
            value_group(0, 0)
            value_group(0, 1)
            with pe.Fori(1, GROUPS // 2 - 1) as pair_lap:
                value_group(pair_lap, 0)
                value_group(pair_lap, 1)
            value_group(GROUPS // 2 - 1, 0)
            value_group(GROUPS // 2 - 1, 1, final=True)
            channel_sum(lambda k: sq_f[:, k], range(KC - 2, KC), KC, 0, 2 * KC + 3 * WC)

        @block.scalar
        def _(act):
            def split_high(lap, j):
                lap, j = lap + j // RING, j % RING
                act.wait_ge(raw_in[j], 16 * (lap + 1))
                if not (isinstance(lap, int) and lap == 0):
                    act.wait_ge(unit_done, RING * (lap - 1) + j + 1)
                nc.scalar.activation(w_hi[:, j, :], raw[:, j, :], ACT.Copy).then_inc(hi_made, 1)

            def take(lap, j, out, func=ACT.Copy):
                act.wait_ge(unit_done, RING * lap + j + 1)
                nc.scalar.activation(halves(out), unit_psum(j), func).then_inc(act_took, 1)

            def root(n, to, scale):
                act.wait_ge(sum_done, n)
                nc.scalar.activation(halves(std[:]), sum_psum(to), ACT.Sqrt, bias=eps[:], scale=scale).then_inc(std_made, 1)

            def mov_high(n0, chunks):
                for n, k in enumerate(chunks):
                    act.wait_ge(nrm_made, n0 + n + 1)
                    nc.scalar.activation(mov_hi[:, k], nrm[:, k], ACT.Copy).then_inc(mov_hi_made, 1)

            act.wait_ge(consts_made, 2)
            for k in range(KC):
                act.wait_ge(x_in[k * XQ // KC], 16)
                nc.scalar.activation(sq[:, k], hid[:, k], ACT.Square).then_inc(sq_made, 1)
            split_high(0, 0)
            split_high(0, 1)
            root(1, 0, 1.0 / D)
            mov_high(0, range(KC))

            def mix_unit(lap, j, func):
                split_high(lap, j + 2)
                out = proj[:, bass.ds(RING * lap + j, 1)].rearrange("p a t -> p (a t)")
                take(lap, j, out, func)

            for lap in range(2 * WC // RING):
                for j in range(RING):
                    mix_unit(lap, j, ACT.Sigmoid if j % 2 else ACT.Copy)
            with act.Fori(2 * WC // RING, N_IN // RING) as lap:
                for j in range(RING):
                    mix_unit(lap, j, ACT.Copy)
            first_out = FIRST_OUT // RING
            split_high(first_out, 2)
            split_high(first_out, 3)
            for c in range(WC):
                act.wait_ge(ya_made, c + 1)
                nc.scalar.activation(sq[:, WC + c], proj[:, 2 * WC + 3 * c], ACT.Square).then_inc(sq_made, 1)
            mov_high(KC, range(WC))
            root(3, 1, 1.0 / WIDTH)
            act.wait_ge(cache_made, 1)
            act.dma_start(caches, cache_out[:]).then_inc(cache_saved, 16)
            for c in range(WC):
                act.wait_ge(centred, c + 1)
                nc.scalar.activation(sq[:, c], proj[:, 2 * c], ACT.Square).then_inc(sq_made, 1)
            split_high(first_out + 1, 0)
            split_high(first_out + 1, 1)
            act.wait_ge(rstd_made, 2)
            root(4, 0, 1.0 / WIDTH)
            for c in range(WC):
                act.wait_ge(scaled_b, c + 1)
                nc.scalar.activation(proj[:, 2 * c + 1], proj[:, 2 * c], ACT.Silu, bias=par_col("conv_norm_b", c),
                                     scale=par_col("conv_norm_g", c)).then_inc(silu_made, 1)
            for c in range(WC):
                act.wait_ge(silu_made, c + 1)
                nc.scalar.activation(sq[:, c], proj[:, 2 * c + 1], ACT.Square).then_inc(sq_made, 1)
            mov_high(KC + WC, range(WC, KC))
            root(5, 1, 1.0 / WIDTH)
            split_high(first_out + 1, 2)
            split_high(first_out + 1, 3)
            for n in range(KC):
                if n in (2, 4):
                    split_high(FIRST_Q // RING, n // 2 - 1)
                act.wait_ge(hid_made, n + 1)
                nc.scalar.activation(sq[:, n], hid[:, n], ACT.Square).then_inc(sq_made, 1)
            root(6, 0, 1.0 / D)
            mov_high(2 * KC, range(KC))

            def take_scores(head):
                act.wait_ge(scores_done, head + 1)
                for b in range(2):
                    nc.scalar.activation(
                        scores[:, bass.ds(head, 1), 2 * b:2 * b + 2, :].rearrange("p a t n -> p (a t n)"),
                        ps_misc[:, b, :], ACT.Copy)
                nc.scalar.activation(
                    scores[0:T_SAMPLE, bass.ds(head, 1), TILES - 1, :].rearrange("p a n -> p (a n)"),
                    ps_misc[0:T_SAMPLE, 2, 0:2 * NKEYS], ACT.Copy).then_inc(scores_took, 1)

            def q_unit(lap, j):
                split_high(FIRST_Q // RING + lap, j + 2)
                take(FIRST_Q // RING + lap, j, q_ring[:, j])

            act.wait_ge(mov_lo_made, 3 * KC)
            act.dma_start(keys[:], sub_keys).then_inc(keys_in, 16)
            for j in range(RING):
                q_unit(0, j)
                if j == 2:
                    take_scores(0)
            with act.Fori(1, N_Q // RING) as lap:
                for j in range(RING):
                    q_unit(lap, j)
                    if j == 0:
                        take_scores(2 * lap - 1)
                    if j == 2:
                        take_scores(2 * lap)

            def spill(lap, j):
                act.wait_ge(act_took, N_IN + N_Q + RING * lap + j + 1)
                dst = acts_dram[bass.ds(RING * lap + j, 1)].rearrange("a p t -> p (a t)")
                act.dma_start(dst, act_ring[:, j % 2]).then_inc(act_saved[j], 16)

            def u_unit(lap, j, first=False, between=None):
                split_high(FIRST_U // RING + lap, j + 2)
                if not first:
                    act.wait_ge(act_saved[(j + 2) % RING], 16 * (lap + j // 2))
                if between:
                    between()
                take(FIRST_U // RING + lap, j, act_ring[:, j % 2], ACT.Gelu)
                spill(lap, j)

            for j in range(RING):
                u_unit(0, j, first=j < 2)
                if j == 0:
                    take_scores(HEADS - 1)
            with act.Fori(1, U_BEFORE) as lap:
                for j in range(RING):
                    u_unit(lap, j)
            act.wait_ge(shifted, 1)
            nc.scalar.activation(gate[:], gate[:], ACT.Exp).then_inc(exp_made, 1)
            for n, dst in enumerate((ij_t[:, 0], ij_t[:, 1], gate_t[:])):
                up = 1.0 if n < 2 else GATE_UP
                act.wait_ge(turned, n + 1)
                nc.scalar.activation(dst[:, 0:T_PROMPT], ps_misc[:, 2 * (n % 2), :], ACT.Copy, scale=up)
                nc.scalar.activation(dst[:, T_PROMPT:T], ps_misc[:, 2 * (n % 2) + 1, 0:T_SAMPLE],
                                     ACT.Copy, scale=up).then_inc(turned_took, 1)

            def take_gates(tg, s, b):
                act.wait_ge(g_done, BATCHES * tg + b + 1)
                nc.scalar.activation(gates[:, s, :, BATCH * b:BATCH * (b + 1)].rearrange("p i t -> p t i"),
                                     ps_misc[:, b % 4, :].rearrange("p (t i) -> p t i", t=BATCH),
                                     ACT.Copy, scale=1.0 / GATE_UP).then_inc(g_took, 1)

            def gate_group(tg, s, first):
                for j in range(RING):
                    def between():
                        if j == 0 and not first:
                            act.wait_ge(g_saved[s], 8 * (tg - s))
                        take_gates(tg, s, 2 * j)
                        take_gates(tg, s, 2 * j + 1)
                    u_unit(U_BEFORE + tg, j, between=between)
                act.wait_ge(g_took, BATCHES * (tg + 1))
                dst = gates_dram[bass.ds(tg, 1)].rearrange("a p i t -> p (a i t)")
                act.dma_start(dst, gates[:, s].rearrange("p i t -> p (i t)")).then_inc(g_saved[s], 16)

            gate_group(0, 0, True)
            gate_group(1, 1, True)
            with act.Fori(1, GTS // 2) as pair_lap:
                gate_group(2 * pair_lap, 0, False)
                gate_group(2 * pair_lap + 1, 1, False)
            gate_group(GTS - 1, 0, False)
            with act.Fori(N_U // RING - U_AFTER, N_U // RING) as lap:
                for j in range(RING):
                    u_unit(lap, j)
            with act.Fori(FIRST_V // RING, N_UNITS // RING - 1) as lap:
                for j in range(RING):
                    split_high(lap, j + 2)
            for n in range(KC):
                if n < 2:
                    split_high(N_UNITS // RING - 1, n + 2)
                act.wait_ge(dve_took, OUTPUTS + N_V - KC + n + 1)
                nc.scalar.activation(sq_f[:, n], hid[:, n], ACT.Square).then_inc(sq_made, 1)
            root(7, 0, 1.0 / D)
            for k in range(KC):
                act.wait_ge(y_made, k + 1)
                act.dma_start(y_t[:, k, :], y_sb[:, k]).then_inc(y_saved, 16)

        @block.vector
        def _(dve):
            count = {"n": 0, "loop": 0}

            def step(ins):
                ins.then_inc(dve_step, 1)
                count["n"] += 1

            def settle():
                dve.wait_ge(dve_step, count["n"] + count["loop"])

            def settle_for_max():
                settle()
                dve.sem_inc(dve_step, 1)
                count["n"] += 1

            def norm_chunks(n_std, src, gains, chunks):
                dve.wait_ge(std_made, n_std)
                nc.vector.reciprocal(rstd[:], std[:]).then_inc(rstd_made, 1)
                dve.wait_ge(rstd_made, n_std)
                for k in chunks:
                    nc.vector.scalar_tensor_tensor(out=nrm[:, k], in0=src(k), scalar=gains(k), in1=rstd[:],
                                                   op0=ALU.mult, op1=ALU.mult).then_inc(nrm_made, 1)

            def mov_low(n0, chunks):
                for n, k in enumerate(chunks):
                    dve.wait_ge(mov_hi_made, n0 + n + 1)
                    dve.wait_ge(nrm_made, n0 + n + 1)
                    nc.vector.tensor_tensor(mov_lo[:, k], nrm[:, k], mov_hi[:, k].bitcast(F32),
                                            ALU.subtract).then_inc(mov_lo_made, 1)

            dve.wait_ge(params_in, 16)
            nc.vector.memset(pad_a[:, :, 0:HIST_A], 0.0)
            nc.vector.memset(pad_b[:, :, 0:HIST_B], 0.0)
            nc.vector.tensor_copy(pad_a[:, :, HIST_A + T_PROMPT:2 * HIST_A + T_PROMPT],
                                  par_col("hist_a", 0, WC * HIST_A).rearrange("p (c n) -> p c n", c=WC))
            step(nc.vector.tensor_copy(pad_b[:, :, HIST_B + T_PROMPT:2 * HIST_B + T_PROMPT],
                                       par_col("hist_b", 0, WC * HIST_B).rearrange("p (c n) -> p c n", c=WC)))
            for q in range(XQ):
                dve.wait_ge(x_in[q], 16)
            norm_chunks(1, lambda k: hid[:, k], lambda k: par_col("mix_g", k), range(KC))
            mov_low(0, range(KC))

            def causal_conv(pad, hist, taps, weight, bias, out, c):
                n = hist + T
                acc = conv[:, 0:n]
                if bias is None:
                    step(nc.vector.tensor_scalar(acc, pad[:, c, 0:n], weight(0), None, ALU.mult))
                else:
                    step(nc.vector.tensor_scalar(acc, pad[:, c, 0:n], weight(0), bias, ALU.mult, ALU.add))
                settle()
                for k in range(1, taps - 1):
                    step(nc.vector.scalar_tensor_tensor(out=acc, in0=pad[:, c, k:k + n], scalar=weight(k), in1=acc,
                                                        op0=ALU.mult, op1=ALU.add))
                    settle()
                for at, to, m in ((0, 0, T_PROMPT), (T_PROMPT + hist, T_PROMPT, T_SAMPLE)):
                    last = nc.vector.scalar_tensor_tensor(
                        out=out[:, to:to + m], in0=pad[:, c, at + taps - 1:at + taps - 1 + m],
                        scalar=weight(taps - 1), in1=conv[:, at:at + m], op0=ALU.mult, op1=ALU.add)
                return last

            for c in range(WC):
                dve.wait_ge(act_took, 2 * c + 2)
                nc.vector.tensor_tensor(pad_b[:, c, HIST_B:HIST_B + T_PROMPT], proj[:, 2 * c, 0:T_PROMPT],
                                        proj[:, 2 * c + 1, 0:T_PROMPT], ALU.mult)
                step(nc.vector.tensor_tensor(pad_b[:, c, 2 * HIST_B + T_PROMPT:PAD_B], proj[:, 2 * c, T_PROMPT:T],
                                             proj[:, 2 * c + 1, T_PROMPT:T], ALU.mult))
                settle()
                causal_conv(pad_b, HIST_B, TAPS_B, lambda k: par_col("conv_b_w", c * TAPS_B + k), par_col("conv_b_b", c),
                            proj[:, 2 * c], c).then_inc(conv_b_made, 1)
            for c in range(WC):
                h, cc, b = (proj[:, 2 * WC + 3 * c + n] for n in range(3))
                dve.wait_ge(act_took, 2 * WC + 3 * c + 3)
                nc.vector.tensor_tensor(pad_a[:, c, HIST_A:HIST_A + T_PROMPT], h[:, 0:T_PROMPT], cc[:, 0:T_PROMPT], ALU.mult)
                step(nc.vector.tensor_tensor(pad_a[:, c, 2 * HIST_A + T_PROMPT:PAD_A], h[:, T_PROMPT:T],
                                             cc[:, T_PROMPT:T], ALU.mult))
                settle()
                step(causal_conv(pad_a, HIST_A, TAPS_A, lambda k: par_col("conv_a_w", c * TAPS_A + k), None, h, c))
                settle()
                nc.vector.tensor_tensor(h, h, b, ALU.mult).then_inc(ya_made, 1)
                dve.wait_ge(ya_made, c + 1)
                nc.vector.tensor_scalar(nrm[:, c], h, par_col("out_a_g", c), None, ALU.mult).then_inc(nrm_made, 1)
            for pad, hist, at in ((pad_a, HIST_A, 0), (pad_b, HIST_B, CACHE_A)):
                out = cache_out[:, at:at + WC * 2 * hist].rearrange("p (c s n) -> p c s n", c=WC, s=2)
                nc.vector.tensor_copy(out[:, :, 0, :], pad[:, :, T_PROMPT:T_PROMPT + hist])
                last = nc.vector.tensor_copy(out[:, :, 1, :], pad[:, :, 2 * hist + T - hist:2 * hist + T])
            last.then_inc(cache_made, 1)
            mov_low(KC, range(WC))
            dve.wait_ge(sum_done, 2)
            mean = conv[:, 0:T]
            step(nc.vector.tensor_scalar(halves(mean), sum_psum(0), 1.0 / WIDTH, None, ALU.mult))
            settle()
            for c in range(WC):
                nc.vector.tensor_tensor(proj[:, 2 * c], proj[:, 2 * c], mean, ALU.subtract).then_inc(centred, 1)

            rstd_a, rstd_b, part = proj[:, 2 * WC + 1], proj[:, 2 * WC + 2], (proj[:, 2 * WC + 4], proj[:, 2 * WC + 5])

            def add_output(q, factor):
                n = FIRST_OUT + q // 2
                if q % 2:
                    dve.wait_ge(unit_done, n + 1)
                else:
                    dve.wait_ge(out_half_done, q // 2 + 1)
                k = q % KC
                nc.vector.tensor_tensor(halves(part[q % 2]), unit_psum(q), halves(factor), ALU.mult).then_inc(dve_took, 1)
                dve.wait_ge(dve_took, q + 1)
                ins = nc.vector.tensor_tensor(hid[:, k], hid[:, k], part[q % 2], ALU.add)
                if q < KC:
                    step(ins)
                else:
                    ins.then_inc(hid_made, 1)

            dve.wait_ge(std_made, 2)
            nc.vector.reciprocal(rstd_a, std[:]).then_inc(rstd_made, 1)
            dve.wait_ge(rstd_made, 2)
            for q in range(WC):
                add_output(q, rstd_a)
            dve.wait_ge(std_made, 3)
            nc.vector.reciprocal(rstd[:], std[:]).then_inc(rstd_made, 1)
            dve.wait_ge(rstd_made, 3)
            dve.wait_ge(centred, WC)
            for c in range(WC):
                nc.vector.tensor_tensor(proj[:, 2 * c], proj[:, 2 * c], rstd[:], ALU.mult).then_inc(scaled_b, 1)
            for q in range(WC, KC):
                add_output(q, rstd_a)
            for c in range(WC):
                dve.wait_ge(silu_made, c + 1)
                nc.vector.tensor_scalar(nrm[:, WC + c], proj[:, 2 * c + 1], par_col("out_b_g", c), None,
                                        ALU.mult).then_inc(nrm_made, 1)
            mov_low(KC + WC, range(WC, KC))
            dve.wait_ge(std_made, 4)
            nc.vector.reciprocal(rstd_b, std[:]).then_inc(rstd_made, 1)
            dve.wait_ge(rstd_made, 4)
            settle()
            for q in range(KC, OUTPUTS):
                add_output(q, rstd_b)
            dve.wait_ge(hid_made, KC)
            norm_chunks(5, lambda k: hid[:, k], lambda k: par_col("ffn_g", k), range(KC))
            mov_low(2 * KC, range(KC))

            dve.wait_ge(iota_made, 1)
            dve.wait_ge(mov_lo_made, 3 * KC)
            step(nc.vector.tensor_copy(iota[:], iota_i[:]))
            settle()
            step(nc.vector.memset(cur[:, TILES - 1], 0.0))
            settle()
            start = count["n"]
            LOWEST = -3.0e38
            with dve.Fori(0, HEADS) as head:
                PER_HEAD = 27
                count["loop"] = head * PER_HEAD
                dve.wait_ge(scores_took, head + 1)
                settle()
                rows = [(t, s) for t in range(TILES) for s in range(2)]

                for t0, t1, rows_in in ((0, TILES - 1, P), (TILES - 1, TILES, T_SAMPLE)):
                    last = nc.vector.tensor_copy(
                        cur[0:rows_in, t0:t1], scores[0:rows_in, bass.ds(head, 1), t0:t1].rearrange("p a t n -> p (a t) n"))
                step(last)
                settle_for_max()
                for t, s in rows:
                    last = nc.vector.max(best[:, t, s, 0:8], cur[:, t, s * NKEYS:(s + 1) * NKEYS])
                step(last)
                settle_for_max()
                for t, s in rows:
                    c = cur[:, t, s * NKEYS:(s + 1) * NKEYS]
                    nc.vector.max_index(best_at[:, t, s, 0:8], best[:, t, s, 0:8], c)
                    last = nc.vector.match_replace(cur[:, t, s * NKEYS:(s + 1) * NKEYS], best[:, t, s, 0:8], c, LOWEST)
                step(last)
                settle_for_max()
                for t, s in rows:
                    last = nc.vector.max(best[:, t, s, 8:16], cur[:, t, s * NKEYS:(s + 1) * NKEYS])
                step(last)
                settle_for_max()
                for t, s in rows:
                    last = nc.vector.max_index(best_at[:, t, s, 8:16], best[:, t, s, 8:16],
                                               cur[:, t, s * NKEYS:(s + 1) * NKEYS])
                step(last)
                shape = [P, TILES, TOPK, TOPK]
                step(nc.vector.tensor_tensor(pair[:], best[:, :, 0, :].unsqueeze(3).broadcast_to(shape),
                                             best[:, :, 1, :].unsqueeze(2).broadcast_to(shape), ALU.add))
                settle_for_max()
                tile_pairs = [pair[:, t].rearrange("p a b -> p (a b)") for t in range(TILES)]
                for t in range(TILES):
                    last = nc.vector.max(top[:, t, 0:8], tile_pairs[t])
                step(last)
                settle_for_max()
                for t in range(TILES):
                    nc.vector.max_index(pair_at[:, t, 0:8], top[:, t, 0:8], tile_pairs[t])
                    last = nc.vector.match_replace(tile_pairs[t], top[:, t, 0:8], tile_pairs[t], LOWEST)
                step(last)
                settle_for_max()
                for t in range(TILES):
                    last = nc.vector.max(top[:, t, 8:16], tile_pairs[t])
                step(last)
                settle_for_max()
                for t in range(TILES):
                    last = nc.vector.max_index(pair_at[:, t, 8:16], top[:, t, 8:16], tile_pairs[t])
                step(last)
                settle()
                spare = cur[:].rearrange("p t (a b) -> p t a b", b=TOPK)
                nc.vector.tensor_copy(tops[:].rearrange("p (t h) k -> p t h k", h=HEADS)[:, :, bass.ds(head, 1), :]
                                      .rearrange("p t a k -> p t (a k)"), top[:])
                nc.vector.tensor_scalar(rank_u[:, 0], pair_at[:], 4, None, ALU.logical_shift_right)
                nc.vector.tensor_scalar(rank_u[:, 1], pair_at[:], TOPK - 1, None, ALU.bitwise_and)
                step(nc.vector.tensor_copy(best_at_f[:], best_at[:]))
                settle()
                step(nc.vector.tensor_copy(rank[:], rank_u[:]))
                settle()
                for s, buf in ((0, pair[:]), (1, spare)):
                    last = nc.vector.tensor_tensor(buf, rank[:, s].unsqueeze(3).broadcast_to(shape),
                                                   iota[:, 0:TOPK].unsqueeze(1).unsqueeze(1).broadcast_to(shape),
                                                   ALU.is_equal)
                step(last)
                settle()
                for s, buf in ((0, pair[:]), (1, spare)):
                    last = nc.vector.tensor_tensor(buf, buf, best_at_f[:, :, s].unsqueeze(2).broadcast_to(shape),
                                                   ALU.mult)
                step(last)
                settle()
                for s, buf in ((0, pair[:]), (1, spare)):
                    last = nc.vector.tensor_reduce(
                        ij[:, s, :, bass.ds(head, 1), :].rearrange("p t a k -> p t (a k)"), buf, AX_X, ALU.add)
                step(last)
                settle()
                while count["n"] - start < PER_HEAD:
                    dve.sem_inc(dve_step, 1)
                    count["n"] += 1
                assert count["n"] - start == PER_HEAD, count["n"] - start
            count["n"] = start + HEADS * PER_HEAD
            count["loop"] = 0
            settle()
            rows = [P, TILES * HEADS, TOPK]
            nc.vector.tensor_tensor(gate[:], tops[:], tops[:, :, 0:1].broadcast_to(rows),
                                    ALU.subtract).then_inc(shifted, 1)
            dve.wait_ge(exp_made, 1)
            step(nc.vector.tensor_reduce(gate_sum[:], gate[:], AX_X, ALU.add))
            settle()
            step(nc.vector.reciprocal(gate_sum[:], gate_sum[:]))
            settle()
            nc.vector.tensor_tensor(gate[:], gate[:], gate_sum[:].unsqueeze(2).broadcast_to(rows),
                                    ALU.mult).then_inc(gate_made, 1)
            dve.wait_ge(turned_took, 3)
            step(nc.vector.tensor_copy(gate_hi[:], gate_t[:]))
            settle()
            step(nc.vector.tensor_tensor(gate_lo[:], gate_t[:], gate_hi[:], ALU.subtract))
            settle()

            hots = [P, BATCH, P]

            def hot_batch(tg, b):
                n, s = BATCHES * tg + b, b % 2
                if not (isinstance(tg, int) and tg == 0 and b < 2):
                    dve.wait_ge(g_done, n - 1)
                at = bass.ds(BATCH * n, BATCH)
                keys_of = iota[:].unsqueeze(1).broadcast_to(hots)
                nc.vector.tensor_tensor(hot_i[:, s], ij_t[:, 0, at].unsqueeze(2).broadcast_to(hots), keys_of,
                                        ALU.is_equal).then_inc(dve_step, 1)
                nc.vector.tensor_tensor(hot_j[:, s], ij_t[:, 1, at].unsqueeze(2).broadcast_to(hots), keys_of,
                                        ALU.is_equal)
                dve.wait_ge(dve_step, hot_start + n + 1)
                nc.vector.tensor_tensor(gated_hi[:, s], hot_i[:, s], gate_hi[:, at].unsqueeze(2).broadcast_to(hots),
                                        ALU.mult)
                nc.vector.tensor_tensor(gated_lo[:, s], hot_i[:, s], gate_lo[:, at].unsqueeze(2).broadcast_to(hots),
                                        ALU.mult).then_inc(hot_made, 1)

            hot_start = count["n"]
            for b in range(BATCHES):
                hot_batch(0, b)
            with dve.Fori(1, GTS) as tg:
                for b in range(BATCHES):
                    hot_batch(tg, b)
            count["n"] += GTS * BATCHES

            prod_start = count["n"]

            def product(pair_lap, s, e):
                g = 2 * pair_lap + s
                n = GROUP * g + e
                half, x = e // 4, e % 4
                if x == 0:
                    dve.wait_ge(gates_back[half], 16 * (g + 1))
                if x % 2 == 0:
                    dve.wait_ge(acts_back[x // 2], 16 * (2 * g + half + 1))
                if not (isinstance(n, int) and n == 0):
                    dve.wait_ge(prod_made, n)
                p = prod[:]
                nc.vector.tensor_tensor(p.rearrange("p (g t) -> p g t", g=GTS),
                                        acts_in[:, x // 2, x % 2].rearrange("p (g t) -> p g t", g=GTS),
                                        gates_in[:, half, :, x, :], ALU.mult).then_inc(dve_step, 1)
                dve.wait_ge(dve_step, prod_start + 2 * n + 1)
                nc.vector.tensor_copy(prod_hi[:, s, e], p).then_inc(dve_step, 1)
                dve.wait_ge(dve_step, prod_start + 2 * n + 2)
                nc.vector.tensor_tensor(prod_lo[:, s, e], p, prod_hi[:, s, e].bitcast(F32),
                                        ALU.subtract).then_inc(prod_made, 1)

            def collect(pair_lap, s, n):
                g = 2 * pair_lap + s
                dve.wait_ge(unit_done, FIRST_V + KC * g + n + 1)
                nc.vector.tensor_tensor(halves(hid[:, n]), halves(hid[:, n]), unit_psum(n), ALU.add).then_inc(dve_took, 1)

            for e in range(GROUP):
                product(0, 0, e)
            with dve.Fori(0, GROUPS // 2 - 1) as pair_lap:
                for s in range(2):
                    for n in range(KC):
                        product(pair_lap + s, 1 - s, n)
                        collect(pair_lap, s, n)
            for n in range(KC):
                product(GROUPS // 2 - 1, 1, n)
                collect(GROUPS // 2 - 1, 0, n)
            for n in range(KC):
                collect(GROUPS // 2 - 1, 1, n)
            count["n"] += 2 * N_U

            dve.wait_ge(dve_took, OUTPUTS + N_V)
            dve.wait_ge(std_made, 6)
            nc.vector.reciprocal(rstd[:], std[:]).then_inc(rstd_made, 1)
            dve.wait_ge(rstd_made, 6)
            for k in range(KC):
                nc.vector.scalar_tensor_tensor(out=y_sb[:, k], in0=hid[:, k], scalar=par_col("final_g", k), in1=rstd[:],
                                               op0=ALU.mult, op1=ALU.mult).then_inc(y_made, 1)


def kernel(x_prompt, x_sample, cache_conv_a, cache_conv_b, norm_mix_g, w_in, conv_a_w, conv_b_w, conv_b_b,
           conv_norm_g, conv_norm_b, out_norm_a_g, out_norm_b_g, w_out, norm_ffn_g, w_q, sub_keys, u_experts,
           v_experts, final_norm_g):
    import numpy as np
    import concourse.bacc as bacc
    from concourse.bass_utils import run_bass_kernel_spmd

    def columns(w):
        w = np.asarray(w).reshape(KC, P, -1, P)
        return w.transpose(2, 1, 0, 3).reshape(-1, P, KC * P)

    def per_channel(a, chunks):
        a = np.asarray(a).reshape(chunks, P, -1)
        return a.transpose(1, 0, 2).reshape(P, -1)

    w_in_units = columns(w_in[0])
    order = [n * WC + c for c in range(WC) for n in (3, 4)] + [n * WC + c for c in range(WC) for n in (0, 1, 2)]
    u = np.asarray(u_experts[0]).reshape(NKEYS, P, KC, P).transpose(0, 3, 2, 1).reshape(N_U, P, KC * P)
    v = np.asarray(v_experts[0]).reshape(GROUPS, GROUP, P, KC, P).transpose(0, 3, 2, 1, 4).reshape(N_V, P, GROUP * P)
    w_out_units = np.asarray(w_out[0]).reshape(2, WC, P, KC // 2, 2, P).transpose(0, 3, 2, 4, 1, 5)
    w_out_units = w_out_units.reshape(N_OUT, P, KC * P)
    stream = np.concatenate([w_in_units[order], w_out_units, columns(w_q[0]), u, v])
    x = np.concatenate([np.asarray(x_prompt[0]), np.asarray(x_sample[0])])
    x_t = np.ascontiguousarray(x.reshape(T, KC, P).transpose(2, 1, 0))
    params = np.concatenate([
        per_channel(norm_mix_g[0], KC), per_channel(norm_ffn_g[0], KC), per_channel(final_norm_g, KC),
        per_channel(np.asarray(conv_a_w[0]).T, WC), per_channel(np.asarray(conv_b_w[0]).T, WC),
        per_channel(conv_b_b[0], WC), per_channel(conv_norm_g[0], WC), per_channel(conv_norm_b[0], WC),
        per_channel(out_norm_a_g[0], WC), per_channel(out_norm_b_g[0], WC),
        per_channel(np.asarray(cache_conv_a[0, 0]).T, WC), per_channel(np.asarray(cache_conv_b[0, 0]).T, WC)], axis=1)
    keys = np.ascontiguousarray(np.asarray(sub_keys[0]).transpose(3, 0, 1, 2).reshape(P, 2 * HEADS, NKEYS))
    arrays = {"stream": stream, "x_t": x_t, "params": np.ascontiguousarray(params), "sub_keys": keys}

    nc = bacc.Bacc("TRN2", target_bir_lowering=False, num_devices=1)
    ins = [nc.dram_tensor(name, a.shape, mybir.dt.from_np(a.dtype), kind="ExternalInput").ap()
           for name, a in arrays.items()]
    y_t = nc.dram_tensor("y_t", (P, KC, T), F32, kind="ExternalOutput").ap()
    caches = nc.dram_tensor("caches", (P, N_CACHE), F32, kind="ExternalOutput").ap()
    build(nc, *ins, y_t, caches)
    got = run_bass_kernel_spmd(nc, [arrays], core_ids=[0]).results[0]
    y = got["y_t"].transpose(2, 1, 0).reshape(T, D)

    def cache(at, hist, which):
        c = got["caches"][:, at:at + WC * 2 * hist].reshape(P, WC, 2, hist)[:, :, which]
        return np.ascontiguousarray(c.transpose(2, 1, 0).reshape(1, 1, hist, WIDTH))

    return (np.ascontiguousarray(y[:T_PROMPT])[None], np.ascontiguousarray(y[T_PROMPT:])[None],
            cache(0, HIST_A, 0), cache(CACHE_A, HIST_B, 0), cache(0, HIST_A, 1), cache(CACHE_A, HIST_B, 1))
```

```python
from contextlib import ExitStack

import concourse.bass as bass
from concourse import mybir

F32 = mybir.dt.float32
F32R = mybir.dt.float32r
U32 = mybir.dt.uint32
I32 = mybir.dt.int32
F16 = mybir.dt.float16
ALU = mybir.AluOpType
ACT = mybir.ActivationFunctionType
AX_X = mybir.AxisListType.X

P = 128
D = 1024
KC = D // P
T_PROMPT, T_SAMPLE = 512, 32
T = T_PROMPT + T_SAMPLE
HALF = T // 2
WIDTH = 512
WC = WIDTH // P
TAPS_A, TAPS_B = 3, 31
HIST_A, HIST_B = TAPS_A - 1, TAPS_B - 1
PAD_A = 2 * HIST_A + T
PAD_B = 2 * HIST_B + T
HEADS, TOPK, NKEYS = 8, 16, 128
TILES = (T + P - 1) // P
EPS = 1e-6
POOL_Y = 3
Y_PIECES = ((POOL_Y, 5), (0, 2), (5, 7), (2, POOL_Y), (7, KC))
POOL_SQ = 3
SQ_X = KC - POOL_SQ
SQ_H = SQ_X + 3 * WC
SQ_Y = SQ_H + KC + 2
XQ = 4

RING = 4
N_IN, N_OUT, N_Q = 5 * WC, KC, 2 * HEADS
N_U = NKEYS
GROUP = 8
GROUPS = NKEYS // GROUP
N_V = GROUPS * KC
OUTPUTS = 2 * KC
FIRST_OUT = N_IN
FIRST_Q = FIRST_OUT + N_OUT
FIRST_U = FIRST_Q + N_Q
FIRST_V = FIRST_U + N_U
N_UNITS = FIRST_V + N_V

GATE_UP = 2.0 ** 14
GT = 32
GTS = T // GT
BATCH = 4
BATCHES = GT // BATCH
U_BEFORE = 11
U_AFTER = N_U // RING - U_BEFORE - GTS

PARAMS = {}
N_PARAMS = 0
for _name, _n in (("mix_g", KC), ("ffn_g", KC), ("final_g", KC), ("conv_a_w", WC * TAPS_A),
                  ("conv_b_w", WC * TAPS_B), ("conv_b_b", WC), ("conv_norm_g", WC), ("conv_norm_b", WC),
                  ("out_a_g", WC), ("out_b_g", WC), ("hist_a", WC * HIST_A), ("hist_b", WC * HIST_B)):
    PARAMS[_name] = N_PARAMS
    N_PARAMS += _n
CACHE_A = WC * 2 * HIST_A
N_CACHE = CACHE_A + WC * 2 * HIST_B


def build(nc, stream, x_t, params, sub_keys, y_t, caches):
    gates_dram = nc.dram_tensor("gates_dram", (GTS, P, NKEYS, GT), F32, kind="Internal").ap()
    acts_dram = nc.dram_tensor("acts_dram", (N_U, P, T), F32, kind="Internal").ap()

    with ExitStack() as ctx:
        def sb_in(stack, name, shape, dt=F32):
            return stack.enter_context(nc.sbuf_tensor(name, shape, dt))

        def sb(name, shape, dt=F32):
            return sb_in(ctx, name, shape, dt)

        def sem(name):
            return ctx.enter_context(nc.semaphore(name))

        par = sb("par", [P, N_PARAMS])
        hid = sb("hid", [P, KC, T])
        mov_hi = sb("mov_hi", [P, KC, T], F32R)
        mov_lo = sb("mov_lo", [P, KC, T], F32R)
        raw = sb("raw", [P, RING, KC * P])
        w_hi = sb("w_hi", [P, RING, KC * P], F32R)
        w_lo = sb("w_lo", [P, RING, KC * P], F32R)
        ones = sb("ones", [P, P])
        eps = sb("eps", [P, 1])
        iota_i = sb("iota_i", [P, P], I32)
        iota = sb("iota", [P, P])
        ident = sb("ident", [P, P])
        std = sb("std", [P, T])
        rstd = sb("rstd", [P, T])
        cache_out = sb("cache_out", [P, N_CACHE])

        mixer = ExitStack()
        proj = sb_in(mixer, "proj", [P, N_IN, T])
        pad_a = sb_in(mixer, "pad_a", [P, WC, PAD_A])
        pad_b = sb_in(mixer, "pad_b", [P, WC, PAD_B])
        conv = sb_in(mixer, "conv", [P, PAD_B])
        nrm = sb_in(mixer, "nrm", [P, KC, T])
        sq = sb_in(mixer, "sq", [P, KC, T])
        mixer.close()

        act_ring = sb("act_ring", [P, 2, T])
        route = ExitStack()
        keys = sb_in(route, "keys", [P, 2 * HEADS, NKEYS])
        ij = sb_in(route, "ij", [P, 2, TILES, HEADS, TOPK])
        tops = sb_in(route, "tops", [P, TILES * HEADS, TOPK])
        gate = sb_in(route, "gate", [P, TILES * HEADS, TOPK])
        gate_sum = sb_in(route, "gate_sum", [P, TILES * HEADS])
        ij_t = sb_in(route, "ij_t", [P, 2, T])
        gate_t = sb_in(route, "gate_t", [P, T])
        gate_hi = sb_in(route, "gate_hi", [P, T], F16)
        gate_lo = sb_in(route, "gate_lo", [P, T])
        topk = ExitStack()
        scores = sb_in(topk, "scores", [P, HEADS, TILES, 2 * NKEYS])
        q_ring = sb_in(topk, "q_ring", [P, RING, T])
        cur = sb_in(topk, "cur", [P, TILES, 2 * NKEYS])
        best = sb_in(topk, "best", [P, TILES, 2, TOPK])
        best_at = sb_in(topk, "best_at", [P, TILES, 2, TOPK], U32)
        best_at_f = sb_in(topk, "best_at_f", [P, TILES, 2, TOPK])
        top = sb_in(topk, "top", [P, TILES, TOPK])
        pair = sb_in(topk, "pair", [P, TILES, TOPK, TOPK])
        pair_at = sb_in(topk, "pair_at", [P, TILES, TOPK], U32)
        rank_u = sb_in(topk, "rank_u", [P, 2, TILES, TOPK], U32)
        rank = sb_in(topk, "rank", [P, 2, TILES, TOPK])
        topk.close()
        build_g = ExitStack()
        gates = sb_in(build_g, "gates", [P, 2, NKEYS, GT])
        hot_j = sb_in(build_g, "hot_j", [P, 2, BATCH, P], F16)
        hot_i = sb_in(build_g, "hot_i", [P, 2, BATCH, P])
        gated_hi = sb_in(build_g, "gated_hi", [P, 2, BATCH, P], F16)
        gated_lo = sb_in(build_g, "gated_lo", [P, 2, BATCH, P], F16)
        build_g.close()
        route.close()

        values = ExitStack()
        acts_in = sb_in(values, "acts_in", [P, 2, 2, T])
        gates_in = sb_in(values, "gates_in", [P, 2, GTS, GROUP // 2, GT])
        prod = sb_in(values, "prod", [P, T])
        prod_hi = sb_in(values, "prod_hi", [P, 2, GROUP, T], F32R)
        prod_lo = sb_in(values, "prod_lo", [P, 2, GROUP, T], F32R)
        values.close()

        final = ExitStack()
        sq_f = sb_in(final, "sq_f", [P, KC, T])
        y_sb = sb_in(final, "y_sb", [P, KC, T])
        final.close()

        ps_unit = ctx.enter_context(nc.psum_tensor("ps_unit", [P, 4, 512], F32))
        ps_misc = ctx.enter_context(nc.psum_tensor("ps_misc", [P, 4, 512], F32))

        params_in = sem("params_in")
        x_in = [sem(f"x_in{q}") for q in range(XQ)]
        keys_in = sem("keys_in")
        raw_in = [sem(f"raw_in{s}") for s in range(RING)]
        hi_made = sem("hi_made")
        lo_made = sem("lo_made")
        unit_done = sem("unit_done")
        act_took = sem("act_took")
        dve_took = sem("dve_took")
        consts_made = sem("consts_made")
        iota_made = sem("iota_made")
        ident_made = sem("ident_made")
        sq_made = sem("sq_made")
        x_sq_made = sem("x_sq_made")
        out_half_done = sem("out_half_done")
        late_out_done = sem("late_out_done")
        hid_made = sem("hid_made")
        sum_done = sem("sum_done")
        std_made = sem("std_made")
        sq_added = sem("sq_added")
        a_added = sem("a_added")
        silu_added = sem("silu_added")
        rstd_made = sem("rstd_made")
        nrm_made = sem("nrm_made")
        mov_hi_made = sem("mov_hi_made")
        mov_lo_made = sem("mov_lo_made")
        low_odd_made = sem("low_odd_made")
        in_scaled = sem("in_scaled")
        sigmoid_made = sem("sigmoid_made")
        pool_step = sem("pool_step")
        pad_a_made = sem("pad_a_made")
        taps_made = sem("taps_made")
        pads_ready = sem("pads_ready")
        conv_b_made = sem("conv_b_made")
        ya_made = sem("ya_made")
        centred = sem("centred")
        scaled_b = sem("scaled_b")
        silu_made = sem("silu_made")
        cache_made = sem("cache_made")
        cache_saved = sem("cache_saved")
        scores_done = sem("scores_done")
        scores_took = sem("scores_took")
        shifted = sem("shifted")
        exp_made = sem("exp_made")
        gate_made = sem("gate_made")
        turned = sem("turned")
        turned_took = sem("turned_took")
        hot_made = sem("hot_made")
        g_done = sem("g_done")
        g_took = sem("g_took")
        g_saved = [sem(f"g_saved{s}") for s in range(2)]
        act_saved = [sem(f"act_saved{s}") for s in range(RING)]
        acts_back = [sem(f"acts_back{s}") for s in range(2)]
        gates_back = [sem(f"gates_back{s}") for s in range(2)]
        prod_made = sem("prod_made")
        dve_step = sem("dve_step")
        late_value_done = sem("late_value_done")
        late_took = sem("late_took")
        y_gained = sem("y_gained")
        y_made_pool = sem("y_made_pool")
        y_made = sem("y_made")
        y_saved = sem("y_saved")

        block = ctx.enter_context(nc.Block())

        def par_col(name, i, n=1):
            return par[:, PARAMS[name] + i:PARAMS[name] + i + n]

        def halves(ap):
            return ap.rearrange("p (a b) -> p a b", a=2)

        def half(ap, a):
            return ap[:, a * HALF:(a + 1) * HALF]

        def unit_psum(j):
            return ps_unit[:, 2 * (j % 2):2 * (j % 2) + 2, 0:HALF]

        def sum_psum(pair_of_banks):
            return ps_misc[:, 2 * pair_of_banks:2 * pair_of_banks + 2, 0:HALF]

        def tap_product(c, k):
            at = (k + TAPS_A * (c % 2)) * PAD_A
            return nrm[:].rearrange("p k t -> p (k t)")[:, at:at + HIST_A + T]

        assert 2 * TAPS_A * PAD_A + PAD_B <= KC * T
        odd_sum = nrm[:].rearrange("p k t -> p (k t)")[:, 2 * TAPS_A * PAD_A:2 * TAPS_A * PAD_A + PAD_B]

        def out_psum(q):
            return sum_psum(q - 2) if q in (2, 3) else unit_psum(q)


        @block.sync
        def _(sp):
            def load(lap, j):
                if not (isinstance(lap, int) and lap == 0):
                    sp.wait_ge(hi_made, RING * (lap - 1) + j + 1)
                    sp.wait_ge(lo_made, RING * (lap - 1) + j + 1)
                src = stream[bass.ds(RING * lap + j, 1)].rearrange("a p n -> p (a n)")
                sp.dma_start(raw[:, j, :], src).then_inc(raw_in[j], 16)

            def load_acts(half, q):
                for n in (2 * q, 2 * q + 1):
                    sp.wait_ge(act_saved[n], 16 * (half + 1))
                acts = acts_dram[bass.ds(4 * half + 2 * q, 2)].rearrange("e p t -> p e t")
                sp.dma_start(acts_in[:, q], acts).then_inc(acts_back[q], 16)

            def load_gates(pair_lap, s):
                g = gates_dram[:, :, bass.ds(4 * (2 * pair_lap + s), 4), :].rearrange("g p e t -> p g (e t)")
                sp.dma_start(gates_in[:, s].rearrange("p g e t -> p g (e t)"), g).then_inc(gates_back[s], 16)

            sp.dma_start(par[:], params).then_inc(params_in, 16)
            load(0, 0)
            for q in range(XQ):
                part = slice(q * KC // XQ, (q + 1) * KC // XQ)
                sp.dma_start(hid[:, part], x_t[:, part]).then_inc(x_in[q], 16)
            for j in range(1, RING):
                load(0, j)
            with sp.Fori(1, FIRST_V // RING - U_AFTER + 1) as lap:
                for j in range(RING):
                    load(lap, j)
            sp.wait_ge(g_saved[0], 16 * ((GTS + 1) // 2))
            sp.wait_ge(g_saved[1], 16 * (GTS // 2))
            load_gates(0, 0)
            first_inputs = {0: (0, 0), 2: (0, 1), 6: (1, 0)}
            for n in range(RING * (U_AFTER - 1)):
                load((FIRST_V // RING - U_AFTER + 1) + n // RING, n % RING)
                if n == 4:
                    load_gates(0, 1)
                if n == 6:
                    sp.wait_ge(prod_made, 2)
                if n in first_inputs:
                    load_acts(*first_inputs[n])

            def value_lap(pair_lap, s, gates_too=True):
                v = 8 * pair_lap + 4 * s
                sp.wait_ge(prod_made, v + 4)
                if gates_too:
                    load_gates(pair_lap + 1, s)
                load_acts(2 * pair_lap + s + 1, 1)
                for j in range(RING):
                    if j == 2 and gates_too:
                        sp.wait_ge(prod_made, v + 6)
                        load_acts(2 * pair_lap + s + 2, 0)
                    load(2 * pair_lap + s + FIRST_V // RING, j)

            with sp.Fori(0, GROUPS - 1) as pair_lap:
                value_lap(pair_lap, 0)
                value_lap(pair_lap, 1)
            value_lap(GROUPS - 1, 0, gates_too=False)
            for j in range(RING):
                load(N_UNITS // RING - 1, j)
            sp.wait_ge(y_saved, 16 * 2 * len(Y_PIECES))
            sp.wait_ge(cache_saved, 16)

        @block.gpsimd
        def _(pool):
            nc.gpsimd.memset(ones[:], 1.0).then_inc(consts_made, 1)
            nc.gpsimd.memset(eps[:], EPS).then_inc(consts_made, 1)
            nc.gpsimd.iota(iota_i[:], [[1, P]], base=0, channel_multiplier=0).then_inc(iota_made, 1)
            nc.gpsimd.memset(ident[:], 0.0).then_inc(ident_made, 1)
            pool.wait_ge(ident_made, 1)
            nc.gpsimd.affine_select(out=ident[:], in_=ident[:], compare_op=ALU.not_equal, fill=1.0, base=0,
                                    pattern=[[-1, P]], channel_multiplier=1).then_inc(ident_made, 1)

            def split_low(lap, j):
                pool.wait_ge(raw_in[j], 16 * (lap + 1))
                pool.wait_ge(hi_made, RING * lap + j + 1)
                if not (isinstance(lap, int) and lap == 0):
                    pool.wait_ge(unit_done, RING * (lap - 1) + j + 1)
                nc.gpsimd.tensor_tensor(w_lo[:, j, :], raw[:, j, :], w_hi[:, j, :].bitcast(F32),
                                        ALU.subtract).then_inc(lo_made, 1)

            steps = [0]

            def step(ins):
                ins.then_inc(pool_step, 1)
                steps[0] += 1
                pool.wait_ge(pool_step, steps[0])

            def times(out, a, b):
                return nc.gpsimd.tensor_tensor(out, a, b, ALU.mult)

            def plus(out, a, b):
                return nc.gpsimd.tensor_tensor(out, a, b, ALU.add)

            rstd_2 = std[:]
            split_low(0, 0)
            for k in range(KC - POOL_SQ, KC):
                pool.wait_ge(x_in[k * XQ // KC], 16)
                times(sq[:, k], hid[:, k], hid[:, k]).then_inc(x_sq_made, 1)
            split_low(0, 1)
            for u in range(N_IN):
                if u == 0:
                    split_low(0, 2)
                    split_low(0, 3)
                    pool.wait_ge(rstd_made, 1)
                elif 1 < u < N_IN - 1:
                    split_low((u + 2) // RING, (u + 2) % RING)
                if u == 2:
                    step(times(rstd_2, rstd[:], rstd[:]))
                c, part = (u - 2 * WC) // 3, (u - 2 * WC) % 3
                pool.wait_ge(act_took, u + 1)
                if u == 0:
                    continue
                if u < 2 * WC:
                    times(proj[:, u], proj[:, u], rstd[:]).then_inc(in_scaled, 1)
                    continue
                h, cc, b = (proj[:, 2 * WC + 3 * c + n] for n in range(3))
                if part == 1:
                    step(times(h, h, rstd_2))
                    pool.wait_ge(pads_ready, 1)
                    times(pad_a[:, c, HIST_A:HIST_A + T_PROMPT], h[:, 0:T_PROMPT], cc[:, 0:T_PROMPT])
                    times(pad_a[:, c, 2 * HIST_A + T_PROMPT:PAD_A], h[:, T_PROMPT:T],
                          cc[:, T_PROMPT:T]).then_inc(pad_a_made, 1)
                if part == 2:
                    times(b, b, rstd[:]).then_inc(pool_step, 1)
                    pool.wait_ge(taps_made, c + 1)
                    taps = [tap_product(c, k) for k in range(TAPS_A)]
                    plus(taps[0], taps[0], taps[1]).then_inc(pool_step, 1)
                    steps[0] += 2
                    pool.wait_ge(pool_step, steps[0])
                    plus(h[:, 0:T_PROMPT], taps[0][:, 0:T_PROMPT], taps[2][:, 0:T_PROMPT])
                    step(plus(h[:, T_PROMPT:T], taps[0][:, HIST_A + T_PROMPT:], taps[2][:, HIST_A + T_PROMPT:]))
                    times(h, h, b).then_inc(ya_made, 1)
            for u in range(N_IN + 1, FIRST_U):
                if u == FIRST_Q + 2:
                    for a in range(2):
                        if a == 1:
                            split_low(u // RING, u % RING)
                        for k in range(1, KC, 2):
                            pool.wait_ge(mov_hi_made, (2 + a) * KC + k + 1)
                            pool.wait_ge(nrm_made, a * KC + k + 1)
                            nc.gpsimd.tensor_tensor(half(mov_lo[:, k], a), half(nrm[:, k], a),
                                                    half(mov_hi[:, k], a).bitcast(F32),
                                                    ALU.subtract).then_inc(low_odd_made, 1)
                else:
                    split_low(u // RING, u % RING)
                if u == FIRST_OUT + RING:
                    for c in range(1, WC):
                        pool.wait_ge(sq_made, SQ_X + 2 * WC + c + 1)
                        ins = plus(sq[:, 0], sq[:, 0], sq[:, c])
                        if c < WC - 1:
                            step(ins)
                    ins.then_inc(silu_added, 1)
            with pool.Fori(FIRST_U // RING, N_UNITS // RING) as lap:
                for j in range(RING):
                    split_low(lap, j)
            pool.wait_ge(y_gained, POOL_Y)
            for a in range(2):
                pool.wait_ge(rstd_made, 7 + a)
                for k in range(POOL_Y):
                    times(half(y_sb[:, k], a), half(y_sb[:, k], a), half(rstd[:], a)).then_inc(y_made_pool, 1)

        @block.tensor
        def _(pe):
            def unit(lap, j, hi, lo, chunk_ready=None):
                u = RING * lap + j
                pe.wait_ge(hi_made, u + 1)
                pe.wait_ge(lo_made, u + 1)
                out = unit_psum(j)
                for k in range(KC):
                    if chunk_ready:
                        chunk_ready(k)
                    for n, (w, m) in enumerate(((w_hi, hi), (w_hi, lo), (w_lo, hi))):
                        for a in range(2):
                            last = nc.tensor.matmul(out[:, a, :], w[:, j, k * P:(k + 1) * P],
                                                    m[:, k, a * HALF:(a + 1) * HALF],
                                                    start=(k == 0 and n == 0), stop=(k == KC - 1 and n == 2))
                last.then_inc(unit_done, 1)

            def channel_sum(src, ks, chunks, to, n_sq=None):
                for k in ks:
                    if n_sq is not None:
                        pe.wait_ge(sq_made, n_sq + k + 1)
                    for a in range(2):
                        last = nc.tensor.matmul(sum_psum(to)[:, a, :], ones[:], src(k)[:, a * HALF:(a + 1) * HALF],
                                                start=(k == 0), stop=(k == chunks - 1))
                    if k == chunks - 1:
                        last.then_inc(sum_done, 1)

            def total(squares, n, last_made, to, halves_of=(0, 1)):
                for src, last_one in ((squares[:, 0], False), (squares[:, KC - 1], True)):
                    if last_one:
                        pe.wait_ge(*last_made)
                    else:
                        pe.wait_ge(sq_added, n)
                    for a in halves_of:
                        last = nc.tensor.matmul(sum_psum(to)[:, a, :], ones[:], half(src, a),
                                                start=not last_one, stop=last_one)
                last.then_inc(sum_done, 1)

            def x_ready(k):
                pe.wait_ge(mov_hi_made, k + 1)
                pe.wait_ge(mov_lo_made, k + 1)

            def squares_ready(k):
                for at, n, made, src in ((2, POOL_SQ, x_sq_made, sq[:, KC - 1]), (KC - 3, 1, sq_added, sq[:, 0])):
                    if k == at:
                        pe.wait_ge(made, n)
                        for a in range(2):
                            last = nc.tensor.matmul(sum_psum(0)[:, a, :], ones[:], half(src, a),
                                                    start=(k == 2), stop=(k != 2))
                        if k != 2:
                            last.then_inc(sum_done, 1)

            pe.wait_ge(consts_made, 2)
            for j in range(RING):
                if j >= 2:
                    pe.wait_ge(act_took, j - 1)
                unit(0, j, mov_hi, mov_lo, (x_ready, squares_ready, None, None)[j])
            with pe.Fori(1, N_IN // RING) as lap:
                for j in range(RING):
                    pe.wait_ge(act_took, RING * lap + j - 1)
                    unit(lap, j, mov_hi, mov_lo)
            def out_unit(group, n):
                j = n % RING
                ready = KC + group * WC if n == 0 else None
                u = FIRST_OUT + group * WC + n
                pe.wait_ge(hi_made, u + 1)
                pe.wait_ge(lo_made, u + 1)
                for o in range(2):
                    q = KC * group + 2 * n + o
                    if q in (2, 3):
                        pe.wait_ge(std_made, 5 - q)
                    elif q > 3:
                        pe.wait_ge(dve_took, q - 3 if q < 6 else q - 1)
                    out = out_psum(q)
                    for k in range(WC):
                        if ready and o == 0:
                            pe.wait_ge(mov_hi_made, ready + k + 1)
                            pe.wait_ge(mov_lo_made, ready + k + 1)
                        for m, (w, mov) in enumerate(((w_hi, mov_hi), (w_hi, mov_lo), (w_lo, mov_hi))):
                            for a in range(2):
                                at = (WC * o + k) * P
                                last = nc.tensor.matmul(out[:, a, :], w[:, j, at:at + P],
                                                        mov[:, WC * group + k, a * HALF:(a + 1) * HALF],
                                                        start=(k == 0 and m == 0), stop=(k == WC - 1 and m == 2))
                    last.then_inc(unit_done if o else out_half_done, 1)

            for c in range(WC):
                pe.wait_ge(conv_b_made, c + 1)
                channel_sum(lambda c: proj[:, 2 * c], (c,), WC, 0)
            channel_sum(lambda c: sq[:, c], range(WC), WC, 1, SQ_X + WC - 1)
            pe.wait_ge(a_added, 1)
            pe.wait_ge(sq_made, SQ_X + 2 * WC)
            channel_sum(lambda n: sq[:, (WC, KC - 1)[n]], range(2), 2, 0)
            pe.wait_ge(act_took, N_IN)
            out_unit(0, 0)
            out_unit(0, 1)
            out_unit(0, 2)
            pe.wait_ge(dve_took, WC)
            pe.wait_ge(silu_added, 1)
            channel_sum(lambda c: sq[:, c], (0,), 1, 1)
            out_unit(0, 3)
            for n in range(WC - 1):
                out_unit(1, n)
            pe.wait_ge(hi_made, FIRST_Q)
            pe.wait_ge(lo_made, FIRST_Q)
            for a in range(2):
                for o in range(2):
                    if a == 0:
                        pe.wait_ge(dve_took, OUTPUTS - 3 + o)
                    for k in range(WC):
                        for m, (w, mov) in enumerate(((w_hi, mov_hi), (w_hi, mov_lo), (w_lo, mov_hi))):
                            at = (WC * o + k) * P
                            last = nc.tensor.matmul(unit_psum(o)[:, a, :], w[:, RING - 1, at:at + P],
                                                    half(mov[:, WC + k], a),
                                                    start=(k == 0 and m == 0), stop=(k == WC - 1 and m == 2))
                    last.then_inc(unit_done if a and o else late_out_done, 1)
            total(sq, 2, (sq_made, SQ_H + KC), 0, (0,))
            total(sq, 3, (sq_made, SQ_H + KC + 2), 0, (1,))
            pe.wait_ge(dve_took, OUTPUTS)

            def first_queries():
                for a in range(2):
                    for j in range(2):
                        if a == 0:
                            pe.wait_ge(hi_made, FIRST_Q + j + 1)
                            pe.wait_ge(lo_made, FIRST_Q + j + 1)
                        for k in range(KC):
                            if j == 0:
                                pe.wait_ge(mov_hi_made, (2 + a) * KC + k + 1)
                                if k % 2:
                                    pe.wait_ge(low_odd_made, (a * KC + k) // 2 + 1)
                                else:
                                    pe.wait_ge(mov_lo_made, 2 * KC + (a * KC + k) // 2 + 1)
                            for m, (w, mov) in enumerate(((w_hi, mov_hi), (w_hi, mov_lo), (w_lo, mov_hi))):
                                last = nc.tensor.matmul(unit_psum(j)[:, a, :], w[:, j, k * P:(k + 1) * P],
                                                        half(mov[:, k], a),
                                                        start=(k == 0 and m == 0), stop=(k == KC - 1 and m == 2))
                        if a == 1:
                            last.then_inc(unit_done, 1)

            def head_scores(head, s):
                pe.wait_ge(act_took, N_IN + 2 * head + 2)
                if not (isinstance(head, int) and head == 0):
                    pe.wait_ge(scores_took, head)
                for t in range(TILES):
                    n = min(P, T - t * P)
                    for side in range(2):
                        last = nc.tensor.matmul(ps_misc[0:n, t // 2, (t % 2) * 256 + side * P:(t % 2) * 256 + side * P + P],
                                                q_ring[:, 2 * s + side, t * P:t * P + n],
                                                key_view(head, s, side), start=True, stop=True)
                last.then_inc(scores_done, 1)

            def key_view(head, s, side):
                return keys[:, bass.ds(2 * head + side, 1), :].rearrange("p a n -> p (a n)")

            first_queries()
            for n in range(2, RING):
                pe.wait_ge(act_took, N_IN + n - 1)
                unit(FIRST_Q // RING, n, mov_hi, mov_lo)
                if n == 2:
                    pe.wait_ge(keys_in, 16)
                    head_scores(0, 0)
            with pe.Fori(1, N_Q // RING) as lap:
                for j in range(RING):
                    pe.wait_ge(act_took, N_IN + RING * lap + j - 1)
                    unit(FIRST_Q // RING + lap, j, mov_hi, mov_lo)
                    if j == 0:
                        head_scores(2 * lap - 1, 1)
                    if j == 2:
                        head_scores(2 * lap, 0)

            def u_unit(lap, j):
                pe.wait_ge(act_took, N_IN + N_Q + RING * lap + j - 1)
                unit(FIRST_U // RING + lap, j, mov_hi, mov_lo)

            for j in range(RING):
                u_unit(0, j)
                if j == 0:
                    head_scores(HEADS - 1, 1)
            with pe.Fori(1, U_BEFORE - 1) as lap:
                for j in range(RING):
                    u_unit(lap, j)

            def turn(n):
                for t in range(TILES):
                    src = ij[:, n, t] if n < 2 else gate[:, t * HEADS:(t + 1) * HEADS]
                    last = nc.tensor.transpose(ps_misc[:, 2 * (n % 2) + t // 4, (t % 4) * P:(t % 4 + 1) * P],
                                               src.rearrange("p h k -> p (h k)"), ident[:])
                last.then_inc(turned, 1)

            for j in range(RING):
                u_unit(U_BEFORE - 1, j)
                if j == 1:
                    pe.wait_ge(gate_made, 1)
                    pe.wait_ge(ident_made, 2)
                    pe.wait_ge(scores_took, HEADS)
                    turn(0)
                    turn(1)
                if j == 2:
                    pe.wait_ge(turned_took, 1)
                    turn(2)
            pe.wait_ge(turned_took, 3)

            def gate_batch(tg, b):
                n = BATCHES * tg + b
                pe.wait_ge(hot_made, n + 1)
                if not (isinstance(tg, int) and tg == 0 and b < 4):
                    pe.wait_ge(g_took, n - 3)
                for x in range(BATCH):
                    for m, g in enumerate((gated_hi, gated_lo)):
                        last = nc.tensor.matmul(ps_misc[:, b % 4, x * P:(x + 1) * P], hot_j[:, b % 2, x],
                                                g[:, b % 2, x], start=(m == 0), stop=(m == 1))
                last.then_inc(g_done, 1)

            def gate_group(tg):
                for j in range(RING):
                    gate_batch(tg, 2 * j)
                    gate_batch(tg, 2 * j + 1)
                    u_unit(tg + U_BEFORE, j)

            gate_group(0)
            with pe.Fori(1, GTS) as tg:
                gate_group(tg)
            with pe.Fori(N_U // RING - U_AFTER, N_U // RING) as lap:
                for j in range(RING):
                    u_unit(lap, j)

            def value_group(pair_lap, s, chunks=KC):
                g = 2 * pair_lap + s
                pe.wait_ge(prod_made, GROUP * (g + 1))
                for n in range(chunks):
                    first = isinstance(pair_lap, int) and pair_lap == 0 and s == 0 and n < 2
                    if not first:
                        pe.wait_ge(dve_took, OUTPUTS + KC * g + n - 1)
                    unit(FIRST_V // RING + 2 * g + n // RING, n % RING, prod_hi[:, s], prod_lo[:, s])

            pe.wait_ge(act_took, N_IN + N_Q + N_U)
            value_group(0, 0)
            value_group(0, 1)
            with pe.Fori(1, GROUPS // 2 - 1) as pair_lap:
                value_group(pair_lap, 0)
                value_group(pair_lap, 1)
            value_group(GROUPS // 2 - 1, 0)
            value_group(GROUPS // 2 - 1, 1, KC - 1)
            pe.wait_ge(dve_took, OUTPUTS + N_V - 2)
            pe.wait_ge(hi_made, N_UNITS)
            pe.wait_ge(lo_made, N_UNITS)
            for a in range(2):
                for k in range(KC):
                    if a == 1 and k == KC - 1:
                        total(sq_f, 4, (sq_made, SQ_Y + KC), 0, (0,))
                    for m, (w, mov) in enumerate(((w_hi, prod_hi), (w_hi, prod_lo), (w_lo, prod_hi))):
                        last = nc.tensor.matmul(unit_psum(KC - 1)[:, a, :], w[:, RING - 1, k * P:(k + 1) * P],
                                                half(mov[:, 1, k], a),
                                                start=(k == 0 and m == 0), stop=(k == KC - 1 and m == 2))
                last.then_inc(unit_done if a else late_value_done, 1)
            total(sq_f, 4, (sq_made, SQ_Y + KC + 1), 0, (1,))

        @block.scalar
        def _(act):
            def split_high(lap, j):
                lap, j = lap + j // RING, j % RING
                act.wait_ge(raw_in[j], 16 * (lap + 1))
                if not (isinstance(lap, int) and lap == 0):
                    act.wait_ge(unit_done, RING * (lap - 1) + j + 1)
                nc.scalar.activation(w_hi[:, j, :], raw[:, j, :], ACT.Copy).then_inc(hi_made, 1)

            def take(lap, j, out, func=ACT.Copy):
                act.wait_ge(unit_done, RING * lap + j + 1)
                nc.scalar.activation(halves(out), unit_psum(j % RING), func).then_inc(act_took, 1)

            def root(n, to, scale):
                act.wait_ge(sum_done, n)
                nc.scalar.activation(halves(std[:]), sum_psum(to), ACT.Sqrt, bias=eps[:], scale=scale).then_inc(std_made, 1)

            split_high(0, 0)
            act.wait_ge(params_in, 16)
            for k in range(KC):
                act.wait_ge(x_in[k * XQ // KC], 16)
                nc.scalar.activation(mov_hi[:, k], hid[:, k], ACT.Copy,
                                     scale=par_col("mix_g", k)).then_inc(mov_hi_made, 1)
            split_high(0, 1)
            for k in range(KC - POOL_SQ):
                nc.scalar.activation(sq[:, k], hid[:, k], ACT.Square).then_inc(sq_made, 1)
            split_high(0, 2)
            split_high(0, 3)
            take(0, 0, proj[:, 0])
            root(1, 0, 1.0 / D)

            def gates_of(c):
                act.wait_ge(in_scaled, 2 * c + 1)
                nc.scalar.activation(proj[:, 2 * c + 1], proj[:, 2 * c + 1], ACT.Sigmoid).then_inc(sigmoid_made, 1)

            def taps_of(c):
                act.wait_ge(pad_a_made, c + 1)
                for k in range(TAPS_A):
                    last = nc.scalar.activation(tap_product(c, k), pad_a[:, c, k:k + HIST_A + T], ACT.Copy,
                                                scale=par_col("conv_a_w", c * TAPS_A + k))
                last.then_inc(taps_made, 1)

            def squares_a(c):
                act.wait_ge(ya_made, c + 1)
                nc.scalar.activation(sq[:, WC + c], proj[:, 2 * WC + 3 * c], ACT.Square).then_inc(sq_made, 1)

            def group_high(c, src, gain):
                nc.scalar.activation(mov_hi[:, c], src, ACT.Copy, scale=gain).then_inc(mov_hi_made, 1)

            for u in range(N_IN):
                c, part = (u - 2 * WC) // 3, (u - 2 * WC) % 3
                if 0 < u < N_IN - 1:
                    split_high(0, u + 3)
                if u > 2 * WC and part == 2:
                    taps_of(c)
                if u > 0:
                    take(0, u, proj[:, u])
                if u == 1:
                    gates_of(0)
                if 4 <= u <= 2 * WC and u % 2 == 0:
                    gates_of(u // 2 - 1)
                if u > 2 * WC and part == 1 and c > 0:
                    squares_a(c - 1)
            first_out = FIRST_OUT // RING
            act.wait_ge(act_took, N_IN)
            for c in range(WC - 1):
                group_high(c, proj[:, 2 * WC + 3 * c], par_col("out_a_g", c))
            for c in range(WC):
                act.wait_ge(centred, c + 1)
                nc.scalar.activation(sq[:, c], proj[:, 2 * c], ACT.Square).then_inc(sq_made, 1)
            act.wait_ge(ya_made, WC)
            group_high(WC - 1, proj[:, 2 * WC + 3 * (WC - 1)], par_col("out_a_g", WC - 1))
            squares_a(WC - 1)
            root(3, 1, 1.0 / WIDTH)
            split_high(first_out, 2)
            split_high(first_out, 3)
            act.wait_ge(rstd_made, 2)
            root(4, 0, 1.0 / WIDTH)
            act.wait_ge(cache_made, 1)
            act.dma_start(caches, cache_out[:]).then_inc(cache_saved, 16)
            for c in range(WC):
                act.wait_ge(scaled_b, c + 1)
                nc.scalar.activation(proj[:, 2 * c + 1], proj[:, 2 * c], ACT.Silu, bias=par_col("conv_norm_b", c),
                                     scale=par_col("conv_norm_g", c)).then_inc(silu_made, 1)
            split_high(first_out + 1, 0)
            for c in range(WC):
                act.wait_ge(silu_made, c + 1)
                nc.scalar.activation(sq[:, c], proj[:, 2 * c + 1], ACT.Square).then_inc(sq_made, 1)
            for c in range(WC):
                group_high(WC + c, proj[:, 2 * c + 1], par_col("out_b_g", c))
            split_high(first_out + 1, 1)
            act.wait_ge(rstd_made, 3)
            root(5, 1, 1.0 / WIDTH)
            split_high(first_out + 1, 2)
            split_high(first_out + 1, 3)
            for n in range(KC):
                if n in (2, 4):
                    split_high(FIRST_Q // RING, n // 2 - 1)
                if n < KC - 2:
                    act.wait_ge(hid_made, n + 1)
                    nc.scalar.activation(sq[:, n], hid[:, n], ACT.Square).then_inc(sq_made, 1)
            for a in range(2):
                for n in (KC - 2, KC - 1):
                    act.wait_ge(hid_made, n + 2 * a + 1)
                    nc.scalar.activation(half(sq[:, n], a), half(hid[:, n], a), ACT.Square).then_inc(sq_made, 1)
            act.wait_ge(rstd_made, 4)
            for a in range(2):
                act.wait_ge(sum_done, 6 + a)
                nc.scalar.activation(half(std[:], a), sum_psum(0)[:, a, :], ACT.Sqrt, bias=eps[:],
                                     scale=1.0 / D).then_inc(std_made, 1)
            for a in range(2):
                if a == 1:
                    split_high(FIRST_Q // RING, 2)
                for k in range(KC):
                    act.wait_ge(nrm_made, a * KC + k + 1)
                    nc.scalar.activation(half(mov_hi[:, k], a), half(nrm[:, k], a), ACT.Copy).then_inc(mov_hi_made, 1)

            def take_scores(head):
                act.wait_ge(scores_done, head + 1)
                for b in range(2):
                    nc.scalar.activation(
                        scores[:, bass.ds(head, 1), 2 * b:2 * b + 2, :].rearrange("p a t n -> p (a t n)"),
                        ps_misc[:, b, :], ACT.Copy)
                nc.scalar.activation(
                    scores[0:T_SAMPLE, bass.ds(head, 1), TILES - 1, :].rearrange("p a n -> p (a n)"),
                    ps_misc[0:T_SAMPLE, 2, 0:2 * NKEYS], ACT.Copy).then_inc(scores_took, 1)

            def q_unit(lap, j, split=True):
                if split:
                    split_high(FIRST_Q // RING + lap, j + 2)
                take(FIRST_Q // RING + lap, j, q_ring[:, j])

            act.wait_ge(mov_lo_made, 3 * KC)
            act.wait_ge(low_odd_made, KC)
            act.dma_start(keys[:], sub_keys).then_inc(keys_in, 16)
            for j in range(RING):
                q_unit(0, j, split=j > 0)
                if j == 2:
                    take_scores(0)
            with act.Fori(1, N_Q // RING) as lap:
                for j in range(RING):
                    q_unit(lap, j)
                    if j == 0:
                        take_scores(2 * lap - 1)
                    if j == 2:
                        take_scores(2 * lap)

            def spill(lap, j):
                act.wait_ge(act_took, N_IN + N_Q + RING * lap + j + 1)
                dst = acts_dram[bass.ds(RING * lap + j, 1)].rearrange("a p t -> p (a t)")
                act.dma_start(dst, act_ring[:, j % 2]).then_inc(act_saved[j], 16)

            def u_unit(lap, j, first=False, between=None):
                split_high(FIRST_U // RING + lap, j + 2)
                if not first:
                    act.wait_ge(act_saved[(j + 2) % RING], 16 * (lap + j // 2))
                if between:
                    between()
                take(FIRST_U // RING + lap, j, act_ring[:, j % 2], ACT.Gelu)
                spill(lap, j)

            for j in range(RING):
                u_unit(0, j, first=j < 2)
                if j == 0:
                    take_scores(HEADS - 1)
            with act.Fori(1, U_BEFORE - 1) as lap:
                for j in range(RING):
                    u_unit(lap, j)
            act.wait_ge(shifted, 1)
            nc.scalar.activation(gate[:], gate[:], ACT.Exp).then_inc(exp_made, 1)

            def take_turned(n, dst, up):
                act.wait_ge(turned, n + 1)
                nc.scalar.activation(dst[:, 0:T_PROMPT], ps_misc[:, 2 * (n % 2), :], ACT.Copy, scale=up)
                nc.scalar.activation(dst[:, T_PROMPT:T], ps_misc[:, 2 * (n % 2) + 1, 0:T_SAMPLE],
                                     ACT.Copy, scale=up).then_inc(turned_took, 1)

            for j in range(RING):
                u_unit(U_BEFORE - 1, j)
                if j == 1:
                    take_turned(0, ij_t[:, 0], 1.0)
                    take_turned(1, ij_t[:, 1], 1.0)
                if j == 2:
                    take_turned(2, gate_t[:], GATE_UP)

            def take_gates(tg, s, b):
                act.wait_ge(g_done, BATCHES * tg + b + 1)
                nc.scalar.activation(gates[:, s, :, BATCH * b:BATCH * (b + 1)].rearrange("p i t -> p t i"),
                                     ps_misc[:, b % 4, :].rearrange("p (t i) -> p t i", t=BATCH),
                                     ACT.Copy, scale=1.0 / GATE_UP).then_inc(g_took, 1)

            def gate_group(tg, s, first):
                for j in range(RING):
                    def between():
                        if j == 0 and not first:
                            act.wait_ge(g_saved[s], 8 * (tg - s))
                        take_gates(tg, s, 2 * j)
                        take_gates(tg, s, 2 * j + 1)
                    u_unit(U_BEFORE + tg, j, between=between)
                act.wait_ge(g_took, BATCHES * (tg + 1))
                dst = gates_dram[bass.ds(tg, 1)].rearrange("a p i t -> p (a i t)")
                act.dma_start(dst, gates[:, s].rearrange("p i t -> p (i t)")).then_inc(g_saved[s], 16)

            gate_group(0, 0, True)
            gate_group(1, 1, True)
            with act.Fori(1, GTS // 2) as pair_lap:
                gate_group(2 * pair_lap, 0, False)
                gate_group(2 * pair_lap + 1, 1, False)
            gate_group(GTS - 1, 0, False)
            with act.Fori(N_U // RING - U_AFTER, N_U // RING) as lap:
                for j in range(RING):
                    u_unit(lap, j)
            with act.Fori(FIRST_V // RING, N_UNITS // RING - 1) as lap:
                for j in range(RING):
                    split_high(lap, j + 2)
            for n in range(KC):
                if n < 2:
                    split_high(N_UNITS // RING - 1, n + 2)
                if n < KC - 1:
                    act.wait_ge(dve_took, OUTPUTS + N_V - KC + n + 1)
                    nc.scalar.activation(sq_f[:, n], hid[:, n], ACT.Square).then_inc(sq_made, 1)
                if n < POOL_Y:
                    nc.scalar.activation(y_sb[:, n], hid[:, n], ACT.Copy, scale=par_col("final_g", n)).then_inc(y_gained, 1)
            for a in range(2):
                act.wait_ge(late_took, a + 1)
                nc.scalar.activation(half(sq_f[:, KC - 1], a), half(hid[:, KC - 1], a), ACT.Square).then_inc(sq_made, 1)
                act.wait_ge(sum_done, 8 + a)
                nc.scalar.activation(half(std[:], a), sum_psum(0)[:, a, :], ACT.Sqrt, bias=eps[:],
                                     scale=1.0 / D).then_inc(std_made, 1)
            for a in range(2):
                for k0, k1 in Y_PIECES:
                    if k0 < POOL_Y:
                        act.wait_ge(y_made_pool, POOL_Y * a + k1)
                    else:
                        act.wait_ge(y_made, (KC - POOL_Y) * a + k1 - POOL_Y)
                    act.dma_start(y_t[:, k0:k1, a * HALF:(a + 1) * HALF],
                                  y_sb[:, k0:k1, a * HALF:(a + 1) * HALF]).then_inc(y_saved, 16)

        @block.vector
        def _(dve):
            count = {"n": 0, "loop": 0}

            def step(ins):
                ins.then_inc(dve_step, 1)
                count["n"] += 1

            def settle():
                dve.wait_ge(dve_step, count["n"] + count["loop"])

            def settle_for_max():
                settle()
                dve.sem_inc(dve_step, 1)
                count["n"] += 1

            def mov_low(n0, k, src, gain):
                dve.wait_ge(mov_hi_made, n0 + 1)
                nc.vector.scalar_tensor_tensor(out=mov_lo[:, k], in0=src, scalar=gain, in1=mov_hi[:, k].bitcast(F32),
                                               op0=ALU.mult, op1=ALU.subtract).then_inc(mov_lo_made, 1)

            def add_square(squares, k, n_sq=None):
                if n_sq:
                    dve.wait_ge(sq_made, n_sq)
                settle()
                ins = nc.vector.tensor_tensor(squares[:, 0], squares[:, 0], squares[:, k], ALU.add)
                if k == KC - 2:
                    ins.then_inc(sq_added, 1)
                else:
                    step(ins)

            def reciprocal(n, out):
                dve.wait_ge(std_made, n)
                nc.vector.reciprocal(out, std[:]).then_inc(rstd_made, 1)

            dve.wait_ge(params_in, 16)
            nc.vector.memset(pad_a[:, :, 0:HIST_A], 0.0)
            nc.vector.memset(pad_b[:, :, 0:HIST_B], 0.0)
            nc.vector.tensor_copy(pad_a[:, :, HIST_A + T_PROMPT:2 * HIST_A + T_PROMPT],
                                  par_col("hist_a", 0, WC * HIST_A).rearrange("p (c n) -> p c n", c=WC))
            nc.vector.tensor_copy(pad_b[:, :, HIST_B + T_PROMPT:2 * HIST_B + T_PROMPT],
                                  par_col("hist_b", 0, WC * HIST_B).rearrange("p (c n) -> p c n", c=WC)
                                  ).then_inc(pads_ready, 1)
            for k in range(KC):
                dve.wait_ge(x_in[k * XQ // KC], 16)
                mov_low(k, k, hid[:, k], par_col("mix_g", k))
            for k in range(1, KC - 1):
                if k < SQ_X:
                    dve.wait_ge(sq_made, k + 1)
                else:
                    dve.wait_ge(x_sq_made, k + 1 - SQ_X)
                add_square(sq, k)
            reciprocal(1, rstd[:])
            dve.wait_ge(pads_ready, 1)

            def conv_b(c):
                n = HIST_B + T

                def tap(k, at=0, m=n):
                    return pad_b[:, c, at + k:at + k + m], par_col("conv_b_w", c * TAPS_B + k)

                sums = (conv[:, 0:n], odd_sum[:, 0:n])
                step(nc.vector.tensor_scalar(sums[0], *tap(0), par_col("conv_b_b", c), ALU.mult, ALU.add))
                step(nc.vector.tensor_scalar(sums[1], *tap(1), None, ALU.mult))
                for k in range(2, TAPS_B - 1):
                    x, w = tap(k)
                    dve.wait_ge(dve_step, count["n"] - 1)
                    step(nc.vector.scalar_tensor_tensor(out=sums[k % 2], in0=x, scalar=w, in1=sums[k % 2],
                                                        op0=ALU.mult, op1=ALU.add))
                settle()
                step(nc.vector.tensor_tensor(sums[0], sums[0], sums[1], ALU.add))
                settle()
                for at, to, m in ((0, 0, T_PROMPT), (T_PROMPT + HIST_B, T_PROMPT, T_SAMPLE)):
                    x, w = tap(TAPS_B - 1, at, m)
                    last = nc.vector.scalar_tensor_tensor(out=proj[:, 2 * c, to:to + m], in0=x, scalar=w,
                                                          in1=conv[:, at:at + m], op0=ALU.mult, op1=ALU.add)
                last.then_inc(conv_b_made, 1)

            for c in range(WC):
                if c == 0:
                    dve.wait_ge(act_took, 1)
                    dve.wait_ge(rstd_made, 1)
                    step(nc.vector.tensor_tensor(proj[:, 0], proj[:, 0], rstd[:], ALU.mult))
                    settle()
                else:
                    dve.wait_ge(in_scaled, 2 * c)
                dve.wait_ge(sigmoid_made, c + 1)
                nc.vector.tensor_tensor(pad_b[:, c, HIST_B:HIST_B + T_PROMPT], proj[:, 2 * c, 0:T_PROMPT],
                                        proj[:, 2 * c + 1, 0:T_PROMPT], ALU.mult)
                step(nc.vector.tensor_tensor(pad_b[:, c, 2 * HIST_B + T_PROMPT:PAD_B], proj[:, 2 * c, T_PROMPT:T],
                                             proj[:, 2 * c + 1, T_PROMPT:T], ALU.mult))
                settle()
                conv_b(c)
            for c in range(WC - 1):
                mov_low(KC + c, c, proj[:, 2 * WC + 3 * c], par_col("out_a_g", c))
            dve.wait_ge(sum_done, 2)
            mean = conv[:, 0:T]
            step(nc.vector.tensor_scalar(halves(mean), sum_psum(0), 1.0 / WIDTH, None, ALU.mult))
            settle()
            for c in range(WC):
                nc.vector.tensor_tensor(proj[:, 2 * c], proj[:, 2 * c], mean, ALU.subtract).then_inc(centred, 1)
            for c in range(1, WC - 1):
                dve.wait_ge(sq_made, SQ_X + c + 1)
                ins = nc.vector.tensor_tensor(sq[:, WC], sq[:, WC], sq[:, WC + c], ALU.add)
                if c < WC - 2:
                    step(ins)
                    settle()
            ins.then_inc(a_added, 1)
            mov_low(KC + WC - 1, WC - 1, proj[:, 2 * WC + 3 * (WC - 1)], par_col("out_a_g", WC - 1))
            dve.wait_ge(pad_a_made, WC)
            for pad, hist, at in ((pad_a, HIST_A, 0), (pad_b, HIST_B, CACHE_A)):
                out = cache_out[:, at:at + WC * 2 * hist].rearrange("p (c s n) -> p c s n", c=WC, s=2)
                nc.vector.tensor_copy(out[:, :, 0, :], pad[:, :, T_PROMPT:T_PROMPT + hist])
                last = nc.vector.tensor_copy(out[:, :, 1, :], pad[:, :, 2 * hist + T - hist:2 * hist + T])
            last.then_inc(cache_made, 1)

            rstd_a, rstd_b, part = proj[:, 2 * WC + 1], proj[:, 2 * WC + 2], (proj[:, 2 * WC + 4], proj[:, 2 * WC + 5])

            def add_output(q, factor):
                n = FIRST_OUT + q // 2
                if q % 2:
                    dve.wait_ge(unit_done, n + 1)
                else:
                    dve.wait_ge(out_half_done, q // 2 + 1)
                k = q % KC
                nc.vector.tensor_tensor(halves(part[q % 2]), out_psum(q), halves(factor), ALU.mult).then_inc(dve_took, 1)
                dve.wait_ge(dve_took, q + 1)
                ins = nc.vector.tensor_tensor(hid[:, k], hid[:, k], part[q % 2], ALU.add)
                if q < KC:
                    step(ins)
                else:
                    ins.then_inc(hid_made, 1)

            reciprocal(2, rstd[:])
            dve.wait_ge(rstd_made, 2)
            dve.wait_ge(centred, WC)
            for c in range(WC):
                nc.vector.tensor_tensor(proj[:, 2 * c], proj[:, 2 * c], rstd[:], ALU.mult).then_inc(scaled_b, 1)
            reciprocal(3, rstd_a)
            dve.wait_ge(rstd_made, 3)
            for q in range(KC - 2):
                add_output(q, rstd_a)
            for c in range(WC):
                mov_low(KC + WC + c, WC + c, proj[:, 2 * c + 1], par_col("out_b_g", c))
            for q in range(KC - 2, KC):
                add_output(q, rstd_a)
            reciprocal(4, rstd_b)
            dve.wait_ge(rstd_made, 4)
            settle()
            for q in range(KC, OUTPUTS - 2):
                add_output(q, rstd_b)
                if q > KC + 1:
                    add_square(sq, q - KC - 1, SQ_H + q - KC)
            add_square(sq, KC - 3, SQ_H + KC - 2)
            settle()
            for a in range(2):
                for o in range(2):
                    k = KC - 2 + o
                    if a and o:
                        dve.wait_ge(unit_done, FIRST_Q)
                    else:
                        dve.wait_ge(late_out_done, 2 * a + o + 1)
                    ins = nc.vector.tensor_tensor(half(part[o], a), unit_psum(o)[:, a, :], half(rstd_b, a), ALU.mult)
                    if a:
                        ins.then_inc(dve_took, 1)
                        dve.wait_ge(dve_took, OUTPUTS - 1 + o)
                    else:
                        step(ins)
                        settle()
                    nc.vector.tensor_tensor(half(hid[:, k], a), half(hid[:, k], a), half(part[o], a),
                                            ALU.add).then_inc(hid_made, 1)
                dve.wait_ge(sq_made, SQ_H + KC - 1 + 2 * a)
                nc.vector.tensor_tensor(half(sq[:, 0], a), half(sq[:, 0], a), half(sq[:, KC - 2], a),
                                        ALU.add).then_inc(sq_added, 1)
            dve.wait_ge(hid_made, KC + 2)
            for a in range(2):
                dve.wait_ge(std_made, 5 + a)
                nc.vector.reciprocal(half(rstd[:], a), half(std[:], a)).then_inc(rstd_made, 1)
                dve.wait_ge(rstd_made, 5 + a)
                for k in range(KC):
                    nc.vector.scalar_tensor_tensor(out=half(nrm[:, k], a), in0=half(hid[:, k], a),
                                                   scalar=par_col("ffn_g", k), in1=half(rstd[:], a),
                                                   op0=ALU.mult, op1=ALU.mult).then_inc(nrm_made, 1)
                    if k % 2:
                        dve.wait_ge(mov_hi_made, (2 + a) * KC + k)
                        dve.wait_ge(nrm_made, a * KC + k)
                        nc.vector.tensor_tensor(half(mov_lo[:, k - 1], a), half(nrm[:, k - 1], a),
                                                half(mov_hi[:, k - 1], a).bitcast(F32),
                                                ALU.subtract).then_inc(mov_lo_made, 1)

            dve.wait_ge(iota_made, 1)
            dve.wait_ge(mov_lo_made, 3 * KC)
            dve.wait_ge(low_odd_made, KC)
            step(nc.vector.tensor_copy(iota[:], iota_i[:]))
            settle()
            step(nc.vector.memset(cur[:, TILES - 1], 0.0))
            settle()
            start = count["n"]
            LOWEST = -3.0e38
            with dve.Fori(0, HEADS) as head:
                PER_HEAD = 27
                count["loop"] = head * PER_HEAD
                dve.wait_ge(scores_took, head + 1)
                settle()
                rows = [(t, s) for t in range(TILES) for s in range(2)]

                for t0, t1, rows_in in ((0, TILES - 1, P), (TILES - 1, TILES, T_SAMPLE)):
                    last = nc.vector.tensor_copy(
                        cur[0:rows_in, t0:t1], scores[0:rows_in, bass.ds(head, 1), t0:t1].rearrange("p a t n -> p (a t) n"))
                step(last)
                settle_for_max()
                for t, s in rows:
                    last = nc.vector.max(best[:, t, s, 0:8], cur[:, t, s * NKEYS:(s + 1) * NKEYS])
                step(last)
                settle_for_max()
                for t, s in rows:
                    c = cur[:, t, s * NKEYS:(s + 1) * NKEYS]
                    nc.vector.max_index(best_at[:, t, s, 0:8], best[:, t, s, 0:8], c)
                    last = nc.vector.match_replace(cur[:, t, s * NKEYS:(s + 1) * NKEYS], best[:, t, s, 0:8], c, LOWEST)
                step(last)
                settle_for_max()
                for t, s in rows:
                    last = nc.vector.max(best[:, t, s, 8:16], cur[:, t, s * NKEYS:(s + 1) * NKEYS])
                step(last)
                settle_for_max()
                for t, s in rows:
                    last = nc.vector.max_index(best_at[:, t, s, 8:16], best[:, t, s, 8:16],
                                               cur[:, t, s * NKEYS:(s + 1) * NKEYS])
                step(last)
                shape = [P, TILES, TOPK, TOPK]
                step(nc.vector.tensor_tensor(pair[:], best[:, :, 0, :].unsqueeze(3).broadcast_to(shape),
                                             best[:, :, 1, :].unsqueeze(2).broadcast_to(shape), ALU.add))
                settle_for_max()
                tile_pairs = [pair[:, t].rearrange("p a b -> p (a b)") for t in range(TILES)]
                for t in range(TILES):
                    last = nc.vector.max(top[:, t, 0:8], tile_pairs[t])
                step(last)
                settle_for_max()
                for t in range(TILES):
                    nc.vector.max_index(pair_at[:, t, 0:8], top[:, t, 0:8], tile_pairs[t])
                    last = nc.vector.match_replace(tile_pairs[t], top[:, t, 0:8], tile_pairs[t], LOWEST)
                step(last)
                settle_for_max()
                for t in range(TILES):
                    last = nc.vector.max(top[:, t, 8:16], tile_pairs[t])
                step(last)
                settle_for_max()
                for t in range(TILES):
                    last = nc.vector.max_index(pair_at[:, t, 8:16], top[:, t, 8:16], tile_pairs[t])
                step(last)
                settle()
                spare = cur[:].rearrange("p t (a b) -> p t a b", b=TOPK)
                nc.vector.tensor_copy(tops[:].rearrange("p (t h) k -> p t h k", h=HEADS)[:, :, bass.ds(head, 1), :]
                                      .rearrange("p t a k -> p t (a k)"), top[:])
                nc.vector.tensor_scalar(rank_u[:, 0], pair_at[:], 4, None, ALU.logical_shift_right)
                nc.vector.tensor_scalar(rank_u[:, 1], pair_at[:], TOPK - 1, None, ALU.bitwise_and)
                step(nc.vector.tensor_copy(best_at_f[:], best_at[:]))
                settle()
                step(nc.vector.tensor_copy(rank[:], rank_u[:]))
                settle()
                for s, buf in ((0, pair[:]), (1, spare)):
                    last = nc.vector.tensor_tensor(buf, rank[:, s].unsqueeze(3).broadcast_to(shape),
                                                   iota[:, 0:TOPK].unsqueeze(1).unsqueeze(1).broadcast_to(shape),
                                                   ALU.is_equal)
                step(last)
                settle()
                for s, buf in ((0, pair[:]), (1, spare)):
                    last = nc.vector.tensor_tensor(buf, buf, best_at_f[:, :, s].unsqueeze(2).broadcast_to(shape),
                                                   ALU.mult)
                step(last)
                settle()
                for s, buf in ((0, pair[:]), (1, spare)):
                    last = nc.vector.tensor_reduce(
                        ij[:, s, :, bass.ds(head, 1), :].rearrange("p t a k -> p t (a k)"), buf, AX_X, ALU.add)
                step(last)
                settle()
                while count["n"] - start < PER_HEAD:
                    dve.sem_inc(dve_step, 1)
                    count["n"] += 1
                assert count["n"] - start == PER_HEAD, count["n"] - start
            count["n"] = start + HEADS * PER_HEAD
            count["loop"] = 0
            settle()
            rows = [P, TILES * HEADS, TOPK]
            nc.vector.tensor_tensor(gate[:], tops[:], tops[:, :, 0:1].broadcast_to(rows),
                                    ALU.subtract).then_inc(shifted, 1)
            dve.wait_ge(exp_made, 1)
            step(nc.vector.tensor_reduce(gate_sum[:], gate[:], AX_X, ALU.add))
            settle()
            step(nc.vector.reciprocal(gate_sum[:], gate_sum[:]))
            settle()
            nc.vector.tensor_tensor(gate[:], gate[:], gate_sum[:].unsqueeze(2).broadcast_to(rows),
                                    ALU.mult).then_inc(gate_made, 1)
            dve.wait_ge(turned_took, 3)
            step(nc.vector.tensor_copy(gate_hi[:], gate_t[:]))
            settle()
            step(nc.vector.tensor_tensor(gate_lo[:], gate_t[:], gate_hi[:], ALU.subtract))
            settle()

            hots = [P, BATCH, P]

            def hot_batch(tg, b):
                n, s = BATCHES * tg + b, b % 2
                if not (isinstance(tg, int) and tg == 0 and b < 2):
                    dve.wait_ge(g_done, n - 1)
                at = bass.ds(BATCH * n, BATCH)
                keys_of = iota[:].unsqueeze(1).broadcast_to(hots)
                nc.vector.tensor_tensor(hot_i[:, s], ij_t[:, 0, at].unsqueeze(2).broadcast_to(hots), keys_of,
                                        ALU.is_equal).then_inc(dve_step, 1)
                nc.vector.tensor_tensor(hot_j[:, s], ij_t[:, 1, at].unsqueeze(2).broadcast_to(hots), keys_of,
                                        ALU.is_equal)
                dve.wait_ge(dve_step, hot_start + n + 1)
                nc.vector.tensor_tensor(gated_hi[:, s], hot_i[:, s], gate_hi[:, at].unsqueeze(2).broadcast_to(hots),
                                        ALU.mult)
                nc.vector.tensor_tensor(gated_lo[:, s], hot_i[:, s], gate_lo[:, at].unsqueeze(2).broadcast_to(hots),
                                        ALU.mult).then_inc(hot_made, 1)

            hot_start = count["n"]
            for b in range(BATCHES):
                hot_batch(0, b)
            with dve.Fori(1, GTS) as tg:
                for b in range(BATCHES):
                    hot_batch(tg, b)
            count["n"] += GTS * BATCHES

            prod_start = count["n"]

            def product(pair_lap, s, e):
                g = 2 * pair_lap + s
                n = GROUP * g + e
                half, x = e // 4, e % 4
                if x == 0:
                    dve.wait_ge(gates_back[half], 16 * (g + 1))
                if x % 2 == 0:
                    dve.wait_ge(acts_back[x // 2], 16 * (2 * g + half + 1))
                if not (isinstance(n, int) and n == 0):
                    dve.wait_ge(prod_made, n)
                p = prod[:]
                nc.vector.tensor_tensor(p.rearrange("p (g t) -> p g t", g=GTS),
                                        acts_in[:, x // 2, x % 2].rearrange("p (g t) -> p g t", g=GTS),
                                        gates_in[:, half, :, x, :], ALU.mult).then_inc(dve_step, 1)
                dve.wait_ge(dve_step, prod_start + 2 * n + 1)
                nc.vector.tensor_copy(prod_hi[:, s, e], p).then_inc(dve_step, 1)
                dve.wait_ge(dve_step, prod_start + 2 * n + 2)
                nc.vector.tensor_tensor(prod_lo[:, s, e], p, prod_hi[:, s, e].bitcast(F32),
                                        ALU.subtract).then_inc(prod_made, 1)

            def collect(pair_lap, s, n):
                g = 2 * pair_lap + s
                dve.wait_ge(unit_done, FIRST_V + KC * g + n + 1)
                nc.vector.tensor_tensor(halves(hid[:, n]), halves(hid[:, n]), unit_psum(n), ALU.add).then_inc(dve_took, 1)

            for e in range(GROUP):
                product(0, 0, e)
            with dve.Fori(0, GROUPS // 2 - 1) as pair_lap:
                for s in range(2):
                    for n in range(KC):
                        product(pair_lap + s, 1 - s, n)
                        collect(pair_lap, s, n)
            for n in range(KC):
                product(GROUPS // 2 - 1, 1, n)
                collect(GROUPS // 2 - 1, 0, n)
            count["n"] += 2 * N_U
            for n in range(KC - 1):
                collect(GROUPS // 2 - 1, 1, n)
                if n > 1:
                    add_square(sq_f, n - 1, SQ_Y + n)
            add_square(sq_f, KC - 2, SQ_Y + KC - 1)
            for a in range(2):
                if a:
                    dve.wait_ge(unit_done, N_UNITS)
                else:
                    dve.wait_ge(late_value_done, 1)
                nc.vector.tensor_tensor(half(hid[:, KC - 1], a), half(hid[:, KC - 1], a), unit_psum(KC - 1)[:, a, :],
                                        ALU.add).then_inc(late_took, 1)

            dve.wait_ge(dve_took, OUTPUTS + N_V - 1)
            dve.wait_ge(late_took, 2)
            for a in range(2):
                dve.wait_ge(std_made, 7 + a)
                nc.vector.reciprocal(half(rstd[:], a), half(std[:], a)).then_inc(rstd_made, 1)
                dve.wait_ge(rstd_made, 7 + a)
                for k in range(POOL_Y, KC):
                    nc.vector.scalar_tensor_tensor(out=half(y_sb[:, k], a), in0=half(hid[:, k], a),
                                                   scalar=par_col("final_g", k), in1=half(rstd[:], a),
                                                   op0=ALU.mult, op1=ALU.mult).then_inc(y_made, 1)


def kernel(x_prompt, x_sample, cache_conv_a, cache_conv_b, norm_mix_g, w_in, conv_a_w, conv_b_w, conv_b_b,
           conv_norm_g, conv_norm_b, out_norm_a_g, out_norm_b_g, w_out, norm_ffn_g, w_q, sub_keys, u_experts,
           v_experts, final_norm_g):
    import numpy as np
    import concourse.bacc as bacc
    from concourse.bass_utils import run_bass_kernel_spmd

    def columns(w):
        w = np.asarray(w).reshape(KC, P, -1, P)
        return w.transpose(2, 1, 0, 3).reshape(-1, P, KC * P)

    def per_channel(a, chunks):
        a = np.asarray(a).reshape(chunks, P, -1)
        return a.transpose(1, 0, 2).reshape(P, -1)

    w_in_units = columns(w_in[0])
    order = [n * WC + c for c in range(WC) for n in (3, 4)] + [n * WC + c for c in range(WC) for n in (0, 1, 2)]
    u = np.asarray(u_experts[0]).reshape(NKEYS, P, KC, P).transpose(0, 3, 2, 1).reshape(N_U, P, KC * P)
    v = np.asarray(v_experts[0]).reshape(GROUPS, GROUP, P, KC, P).transpose(0, 3, 2, 1, 4).reshape(N_V, P, GROUP * P)
    w_out_units = np.asarray(w_out[0]).reshape(2, WC, P, KC // 2, 2, P).transpose(0, 3, 2, 4, 1, 5)
    w_out_units = w_out_units.reshape(N_OUT, P, KC * P)
    stream = np.concatenate([w_in_units[order], w_out_units, columns(w_q[0]), u, v])
    x = np.concatenate([np.asarray(x_prompt[0]), np.asarray(x_sample[0])])
    x_t = np.ascontiguousarray(x.reshape(T, KC, P).transpose(2, 1, 0))
    params = np.concatenate([
        per_channel(norm_mix_g[0], KC), per_channel(norm_ffn_g[0], KC), per_channel(final_norm_g, KC),
        per_channel(np.asarray(conv_a_w[0]).T, WC), per_channel(np.asarray(conv_b_w[0]).T, WC),
        per_channel(conv_b_b[0], WC), per_channel(conv_norm_g[0], WC), per_channel(conv_norm_b[0], WC),
        per_channel(out_norm_a_g[0], WC), per_channel(out_norm_b_g[0], WC),
        per_channel(np.asarray(cache_conv_a[0, 0]).T, WC), per_channel(np.asarray(cache_conv_b[0, 0]).T, WC)], axis=1)
    keys = np.ascontiguousarray(np.asarray(sub_keys[0]).transpose(3, 0, 1, 2).reshape(P, 2 * HEADS, NKEYS))
    arrays = {"stream": stream, "x_t": x_t, "params": np.ascontiguousarray(params), "sub_keys": keys}

    nc = bacc.Bacc("TRN2", target_bir_lowering=False, num_devices=1)
    ins = [nc.dram_tensor(name, a.shape, mybir.dt.from_np(a.dtype), kind="ExternalInput").ap()
           for name, a in arrays.items()]
    y_t = nc.dram_tensor("y_t", (P, KC, T), F32, kind="ExternalOutput").ap()
    caches = nc.dram_tensor("caches", (P, N_CACHE), F32, kind="ExternalOutput").ap()
    build(nc, *ins, y_t, caches)
    got = run_bass_kernel_spmd(nc, [arrays], core_ids=[0]).results[0]
    y = got["y_t"].transpose(2, 1, 0).reshape(T, D)

    def cache(at, hist, which):
        c = got["caches"][:, at:at + WC * 2 * hist].reshape(P, WC, 2, hist)[:, :, which]
        return np.ascontiguousarray(c.transpose(2, 1, 0).reshape(1, 1, hist, WIDTH))

    return (np.ascontiguousarray(y[:T_PROMPT])[None], np.ascontiguousarray(y[T_PROMPT:])[None],
            cache(0, HIST_A, 0), cache(CACHE_A, HIST_B, 0), cache(0, HIST_A, 1), cache(CACHE_A, HIST_B, 1))
```
